# Optimizing a Trainium2 kernel written in Bass

```python
import jax, jax.numpy as jnp
from jax import lax
import numpy as np

D_MODEL = 1024
BATCH = 1
SEQ = 256
DEPTH = 1
DEC_BATCH = 8
DEC_SEQ = 1
PAST_LEN = 2048
PAGE_SIZE = 128

GLA_HEADS = 4
GLA_KEY_WIDTH = D_MODEL // 2
GLA_VAL_WIDTH = D_MODEL
GLA_DK = GLA_KEY_WIDTH // GLA_HEADS
GLA_DV = GLA_VAL_WIDTH // GLA_HEADS
GLA_GATE_RANK = 16
GLA_GATE_TAU = 16.0
GLA_CHUNK = 64
RG_WIDTH = D_MODEL
RG_BLOCKS = 8
RG_BLOCK_W = RG_WIDTH // RG_BLOCKS
CONV_W = 4
RG_C = 8.0
N_BRANCH = 2
N_IN = 2 * GLA_KEY_WIDTH + 2 * GLA_VAL_WIDTH + GLA_GATE_RANK + RG_WIDTH + N_BRANCH * D_MODEL
N_EXPERTS = 32
TOP_K = 4
D_EXPERT = D_MODEL
SWIGLU_LIMIT = 7.0
SWIGLU_ALPHA = 1.702
MOE_BLOCK = 128
DEEPNORM_ALPHA = (2.0 * DEPTH) ** 0.25
DEEPNORM_BETA = (8.0 * DEPTH) ** -0.25
LN_EPS = 1e-5

kernel_name = 'gla_rglru_moe_deepnorm_step'

def _layernorm(x, g, b):
    xf = x.astype(jnp.float32)
    mu = jnp.mean(xf, axis=-1, keepdims=True)
    var = jnp.mean(jnp.square(xf - mu), axis=-1, keepdims=True)
    return ((xf - mu) * lax.rsqrt(var + LN_EPS) * g.astype(jnp.float32) + b.astype(jnp.float32)).astype(x.dtype)

def _gla(q, k, v, log_a, s0):
    n_b, s_len, n_h, _ = q.shape
    dv = v.shape[-1]
    c = min(GLA_CHUNK, s_len)
    n_chunks = -(-s_len // c)
    pad = n_chunks * c - s_len

    def to_chunks(t):
        t = jnp.pad(t, ((0, 0), (0, pad), (0, 0), (0, 0)))
        return t.reshape(n_b, n_chunks, c, n_h, t.shape[-1]).transpose(1, 0, 3, 2, 4)

    mask = jnp.tril(jnp.ones((c, c), dtype=bool))

    def step(state, chunk):
        qc, kc, vc, gc = chunk
        b = jnp.cumsum(gc, axis=2)
        b_last = b[:, :, -1:, :]
        q_e = qc * jnp.exp(b)
        k_e = kc * jnp.exp(-b)
        scores = jnp.where(mask, jnp.einsum('bhtd,bhsd->bhts', q_e, k_e), 0.0)
        o = jnp.einsum('bhts,bhsv->bhtv', scores, vc) + jnp.einsum('bhtd,bhdv->bhtv', q_e, state)
        state = jnp.exp(b_last)[:, :, 0, :, None] * state + jnp.einsum('bhsd,bhsv->bhdv', kc * jnp.exp(b_last - b), vc)
        return state, o

    s_final, o = lax.scan(step, s0, (to_chunks(q), to_chunks(k), to_chunks(v), to_chunks(log_a)))
    o = o.transpose(1, 0, 3, 2, 4).reshape(n_b, n_chunks * c, n_h, dv)[:, :s_len]
    return o, s_final

def _rglru_scan(a, bx, h0):
    def combine(l, r):
        a_l, b_l = l
        a_r, b_r = r
        return a_l * a_r, a_r * b_l + b_r
    a_cum, h = lax.associative_scan(combine, (a, bx), axis=1)
    h = h + a_cum * h0[:, None, :]
    return h, h[:, -1]

def _token_mixers(x, s_gla, h0, conv_buf, w_in, gla_w_a2, gla_b_a, gla_norm_g, rg_conv_w, rg_conv_b,
                  rg_w_a, rg_b_a, rg_w_x, rg_b_x, rg_lambda, b_merge, w_branch, w_o):
    f32 = jnp.float32
    n_b, s_len, _ = x.shape
    proj = jnp.einsum('bsd,dn->bsn', x, w_in)
    cuts = (GLA_KEY_WIDTH, 2 * GLA_KEY_WIDTH, 2 * GLA_KEY_WIDTH + GLA_VAL_WIDTH,
            2 * GLA_KEY_WIDTH + 2 * GLA_VAL_WIDTH, 2 * GLA_KEY_WIDTH + 2 * GLA_VAL_WIDTH + GLA_GATE_RANK,
            2 * GLA_KEY_WIDTH + 2 * GLA_VAL_WIDTH + GLA_GATE_RANK + RG_WIDTH)
    q, k, v, g_out, a_low, xr, merge = jnp.split(proj, cuts, axis=-1)

    q = q.astype(f32).reshape(n_b, s_len, GLA_HEADS, GLA_DK) * (GLA_DK ** -0.5)
    k = k.astype(f32).reshape(n_b, s_len, GLA_HEADS, GLA_DK)
    v = v.astype(f32).reshape(n_b, s_len, GLA_HEADS, GLA_DV)
    log_a = jax.nn.log_sigmoid((a_low @ gla_w_a2 + gla_b_a).astype(f32)) / GLA_GATE_TAU
    o, s_gla_new = _gla(q, k, v, log_a.reshape(n_b, s_len, GLA_HEADS, GLA_DK), s_gla.astype(f32))
    mu = jnp.mean(o, axis=-1, keepdims=True)
    var = jnp.mean(jnp.square(o - mu), axis=-1, keepdims=True)
    o = (o - mu) * lax.rsqrt(var + LN_EPS) * gla_norm_g.astype(f32).reshape(GLA_HEADS, GLA_DV)
    o = o.reshape(n_b, s_len, GLA_VAL_WIDTH) * jax.nn.silu(g_out.astype(f32))

    conv_in = jnp.concatenate([conv_buf.astype(xr.dtype), xr], axis=1)
    xc = rg_conv_b.astype(f32) + sum(conv_in[:, j:j + s_len].astype(f32) * rg_conv_w[j].astype(f32)
                                     for j in range(CONV_W))
    conv_new = conv_in[:, s_len:]
    xb = xc.reshape(n_b, s_len, RG_BLOCKS, RG_BLOCK_W)
    r = jax.nn.sigmoid(jnp.einsum('bsnc,ncd->bsnd', xb, rg_w_a.astype(f32)).reshape(n_b, s_len, RG_WIDTH) + rg_b_a)
    i = jax.nn.sigmoid(jnp.einsum('bsnc,ncd->bsnd', xb, rg_w_x.astype(f32)).reshape(n_b, s_len, RG_WIDTH) + rg_b_x)
    log_a_rg = -RG_C * r * jax.nn.softplus(-rg_lambda.astype(f32))
    a = jnp.exp(log_a_rg)
    bx = jnp.sqrt(-jnp.expm1(2.0 * log_a_rg)) * (i * xc)
    h, h_new = _rglru_scan(a, bx, h0.astype(f32))

    gate_gla, gate_rg = jnp.split(jax.nn.sigmoid((merge + b_merge).astype(f32)), N_BRANCH, axis=-1)
    merged = (gate_gla * jnp.einsum('bsv,vd->bsd', o.astype(x.dtype), w_branch[0])
              + gate_rg * jnp.einsum('bsv,vd->bsd', h.astype(x.dtype), w_branch[1]))
    out = jnp.einsum('bsd,de->bse', merged.astype(x.dtype), w_o)
    return out, s_gla_new, h_new, conv_new

def _moe(x2d, router_w, router_b, moe_w_gu, moe_b_gu, moe_w_down, moe_b_down):
    f32 = jnp.float32
    n_tok, d = x2d.shape
    m = n_tok * TOP_K
    logits = jnp.dot(x2d.astype(f32), router_w.astype(f32)) + router_b.astype(f32)
    top_val, top_idx = lax.top_k(logits, TOP_K)
    top_w = jax.nn.softmax(top_val, axis=-1)
    flat_e = top_idx.reshape(-1).astype(jnp.int32)
    flat_tok = jnp.repeat(jnp.arange(n_tok, dtype=jnp.int32), TOP_K)
    flat_w = top_w.reshape(-1)
    order = jnp.argsort(flat_e)
    e_sorted = flat_e[order]
    counts = jnp.bincount(flat_e, length=N_EXPERTS).astype(jnp.int32)
    padded = (counts + MOE_BLOCK - 1) // MOE_BLOCK * MOE_BLOCK
    start_sorted = jnp.cumsum(counts) - counts
    ends_pad = jnp.cumsum(padded)
    start_pad = ends_pad - padded
    dest = start_pad[e_sorted] + jnp.arange(m, dtype=jnp.int32) - start_sorted[e_sorted]
    n_blocks = -(-m // MOE_BLOCK) + N_EXPERTS
    n_rows = n_blocks * MOE_BLOCK
    row_tok = jnp.full((n_rows,), n_tok, jnp.int32).at[dest].set(flat_tok[order])
    row_w = jnp.zeros((n_rows,), f32).at[dest].set(flat_w[order])
    block_e = jnp.minimum(jnp.searchsorted(ends_pad, jnp.arange(n_blocks, dtype=jnp.int32) * MOE_BLOCK, side='right'),
                          N_EXPERTS - 1)
    x_pad = jnp.concatenate([x2d, jnp.zeros((1, d), x2d.dtype)], axis=0)

    def expert_block(args):
        e, tok = args
        xb = x_pad[tok]
        hgu = xb @ moe_w_gu[e] + moe_b_gu[e]
        gate, up = hgu[:, :D_EXPERT], hgu[:, D_EXPERT:]
        gate = jnp.minimum(gate, SWIGLU_LIMIT)
        up = jnp.clip(up, -SWIGLU_LIMIT, SWIGLU_LIMIT)
        act = (up + 1.0) * gate * jax.nn.sigmoid(SWIGLU_ALPHA * gate)
        return act @ moe_w_down[e] + moe_b_down[e]

    out = lax.map(expert_block, (block_e, row_tok.reshape(n_blocks, MOE_BLOCK)))
    y = jnp.zeros((n_tok + 1, d), f32).at[row_tok].add(row_w[:, None] * out.reshape(n_rows, d).astype(f32))
    return y[:n_tok].astype(x2d.dtype)

def _decoder_layer(x, s_gla, h0, conv_buf, ln1_g, ln1_b, w_in, gla_w_a2, gla_b_a, gla_norm_g, rg_conv_w,
                   rg_conv_b, rg_w_a, rg_b_a, rg_w_x, rg_b_x, rg_lambda, b_merge, w_branch, w_o, ln2_g, ln2_b,
                   router_w, router_b, moe_w_gu, moe_b_gu, moe_w_down, moe_b_down):
    mix, s_gla_new, h_new, conv_new = _token_mixers(
        x, s_gla, h0, conv_buf, w_in, gla_w_a2, gla_b_a, gla_norm_g, rg_conv_w, rg_conv_b,
        rg_w_a, rg_b_a, rg_w_x, rg_b_x, rg_lambda, b_merge, w_branch, w_o)
    x = _layernorm(DEEPNORM_ALPHA * x + mix, ln1_g, ln1_b)
    n_b, s_len, d = x.shape
    ffn = _moe(x.reshape(n_b * s_len, d), router_w, router_b, moe_w_gu, moe_b_gu, moe_w_down, moe_b_down)
    x = _layernorm(DEEPNORM_ALPHA * x + ffn.reshape(n_b, s_len, d), ln2_g, ln2_b)
    return x, s_gla_new, h_new, conv_new

def setup_inputs(seed: int = 0) -> dict:
    key = jax.random.key(seed)
    ks = jax.random.split(key, 32)
    f32 = jnp.float32
    L, D, E, F = DEPTH, D_MODEL, N_EXPERTS, D_EXPERT

    def nrm(k, shape, scale):
        return jax.random.normal(k, shape, f32) * scale

    u = jax.random.uniform(ks[17], (L, RG_WIDTH), f32, 0.9, 0.999)
    s = u ** (1.0 / RG_C)
    rg_lambda = jnp.log(s) - jnp.log1p(-s)
    return {
        'x_prompt': nrm(ks[0], (BATCH, SEQ, D), 1.0),
        'x_sample': nrm(ks[1], (DEC_BATCH, DEC_SEQ, D), 1.0),
        'state_gla': nrm(ks[2], (L, DEC_BATCH, GLA_HEADS, GLA_DK, GLA_DV), 0.1),
        'state_rglru': nrm(ks[3], (L, DEC_BATCH, RG_WIDTH), 0.5),
        'state_conv': nrm(ks[4], (L, DEC_BATCH, CONV_W - 1, RG_WIDTH), 1.0),
        'ln1_g': 1.0 + nrm(ks[5], (L, D), 0.02),
        'ln1_b': nrm(ks[6], (L, D), 0.02),
        'w_in': nrm(ks[7], (L, D, N_IN), D ** -0.5),
        'gla_w_a2': nrm(ks[8], (L, GLA_GATE_RANK, GLA_KEY_WIDTH), GLA_GATE_RANK ** -0.5),
        'gla_b_a': nrm(ks[9], (L, GLA_KEY_WIDTH), 0.1),
        'gla_norm_g': 1.0 + nrm(ks[10], (L, GLA_VAL_WIDTH), 0.02),
        'rg_conv_w': nrm(ks[11], (L, CONV_W, RG_WIDTH), CONV_W ** -0.5),
        'rg_conv_b': nrm(ks[12], (L, RG_WIDTH), 0.02),
        'rg_w_a': nrm(ks[13], (L, RG_BLOCKS, RG_BLOCK_W, RG_BLOCK_W), RG_BLOCK_W ** -0.5),
        'rg_b_a': nrm(ks[14], (L, RG_WIDTH), 0.02),
        'rg_w_x': nrm(ks[15], (L, RG_BLOCKS, RG_BLOCK_W, RG_BLOCK_W), RG_BLOCK_W ** -0.5),
        'rg_b_x': nrm(ks[16], (L, RG_WIDTH), 0.02),
        'rg_lambda': rg_lambda,
        'b_merge': nrm(ks[18], (L, N_BRANCH * D), 0.02),
        'w_branch': nrm(ks[19], (L, N_BRANCH, GLA_VAL_WIDTH, D), GLA_VAL_WIDTH ** -0.5),
        'w_o': nrm(ks[20], (L, D, D), D ** -0.5 * DEEPNORM_BETA),
        'ln2_g': 1.0 + nrm(ks[21], (L, D), 0.02),
        'ln2_b': nrm(ks[22], (L, D), 0.02),
        'router_w': nrm(ks[23], (L, D, E), D ** -0.5),
        'router_b': nrm(ks[24], (L, E), 0.01),
        'moe_w_gu': nrm(ks[25], (L, E, D, 2 * F), D ** -0.5),
        'moe_b_gu': nrm(ks[26], (L, E, 2 * F), 0.02),
        'moe_w_down': nrm(ks[27], (L, E, F, D), F ** -0.5 * DEEPNORM_BETA),
        'moe_b_down': nrm(ks[28], (L, E, D), 0.02),
    }

def reference(x_prompt, x_sample, state_gla, state_rglru, state_conv, ln1_g, ln1_b, w_in, gla_w_a2, gla_b_a,
              gla_norm_g, rg_conv_w, rg_conv_b, rg_w_a, rg_b_a, rg_w_x, rg_b_x, rg_lambda, b_merge, w_branch, w_o,
              ln2_g, ln2_b, router_w, router_b, moe_w_gu, moe_b_gu, moe_w_down, moe_b_down):
    n_prompt = x_prompt.shape[0]
    xp, xs = x_prompt, x_sample
    gla_p, rg_p, conv_p, gla_s, rg_s, conv_s = [], [], [], [], [], []
    for layer in range(DEPTH):
        params = (ln1_g[layer], ln1_b[layer], w_in[layer], gla_w_a2[layer], gla_b_a[layer], gla_norm_g[layer],
                  rg_conv_w[layer], rg_conv_b[layer], rg_w_a[layer], rg_b_a[layer], rg_w_x[layer], rg_b_x[layer],
                  rg_lambda[layer], b_merge[layer], w_branch[layer], w_o[layer], ln2_g[layer], ln2_b[layer],
                  router_w[layer], router_b[layer], moe_w_gu[layer], moe_b_gu[layer], moe_w_down[layer],
                  moe_b_down[layer])
        xp, g_new, h_new, c_new = _decoder_layer(
            xp, jnp.zeros((n_prompt, GLA_HEADS, GLA_DK, GLA_DV), jnp.float32),
            jnp.zeros((n_prompt, RG_WIDTH), jnp.float32),
            jnp.zeros((n_prompt, CONV_W - 1, RG_WIDTH), x_prompt.dtype), *params)
        gla_p.append(g_new)
        rg_p.append(h_new)
        conv_p.append(c_new)
        xs, g_new, h_new, c_new = _decoder_layer(
            xs, state_gla[layer], state_rglru[layer], state_conv[layer], *params)
        gla_s.append(g_new)
        rg_s.append(h_new)
        conv_s.append(c_new)
    return (xp, xs, jnp.stack(gla_p), jnp.stack(rg_p), jnp.stack(conv_p),
            jnp.stack(gla_s), jnp.stack(rg_s), jnp.stack(conv_s))


_drawn_inputs = setup_inputs


def setup_inputs(seed=0):
    import zlib

    import numpy as np

    out = dict(_drawn_inputs(seed))
    spreads = {}
    factors = {'gla_norm_g': 5.151,
     'rg_b_a': 8.0,
     'rg_b_x': 7.833,
     'b_merge': 8.0,
     'ln2_g': 7.534,
     'ln2_b': 7.758,
     'moe_b_gu': 8.0,
     'moe_b_down': 6.101,
     'router_b': 3.344}
    for name, (base, spread) in spreads.items():
        noise = np.random.default_rng([zlib.crc32(name.encode()), seed]).standard_normal(out[name].shape)
        drawn = base * np.exp(spread * noise) if base else spread * noise
        out[name] = __import__('jax').numpy.asarray(drawn.astype(out[name].dtype))
    for name, factor in factors.items():
        out[name] = (out[name] * factor).astype(out[name].dtype)
    return out
```

```python
from contextlib import ExitStack

import concourse.bass as bass
from concourse import mybir

F32 = mybir.dt.float32
BF16 = mybir.dt.bfloat16
I32 = mybir.dt.int32
ALU = mybir.AluOpType
ACT = mybir.ActivationFunctionType
AX_X = mybir.AxisListType.X

P = 128
D = 1024
NB = D // P
SEQ, DEC = 256, 8
T = SEQ + DEC
H, DK, DV = 4, 128, 256
CH = 64
NCH = SEQ // CH
RANK = 16
CW = 4
CIN = CW - 1 + SEQ + DEC * CW
COUT = CIN - (CW - 1)
E = 32
CAP = 64
PAIRS = E // 2
PASSES = -(-T // CAP)
F = D
ALPHA = 2.0 ** 0.25
EPS = 1e-5
LIMIT, SWISH = 7.0, 1.702
TILES = [(0, P), (P, P), (2 * P, DEC)]
NT = len(TILES)
FAR = 4096.0
WCOL = 256
SLOT = NB * T

PACK = {}
_at = 0
for _n, _w in (("conv_w", NB * CW), ("conv_b", NB), ("b_r", NB), ("b_i", NB), ("lam", NB), ("b_a", H),
               ("norm_g", NB), ("b_merge", 2 * NB), ("h0", NB * DEC), ("conv0", NB * DEC * (CW - 1)),
               ("router_w", NB * E), ("ln1_g", NB), ("ln1_b", NB)):
    PACK[_n] = (_at, _w)
    _at += _w
NPACK = _at
OUT_CONVP, OUT_CONVS, OUT_HP, OUT_HS = 0, 24, 24 + 192, 24 + 192 + 8
NOUT = OUT_HS + NB * DEC


def mixer_jobs():
    jobs = [f"xr{n}" for n in range(NB)] + ["low"]
    jobs += [f"k{n}" for n in range(H)]
    for n in range(NB):
        jobs += [f"r{n}", f"i{n}"]
    jobs += [f"q{n}" for n in range(H)] + [f"v{n}" for n in range(NB)]
    jobs += [f"z{n}" for n in range(H)] + [f"g{n}" for n in range(NB)]
    jobs += [f"vt{t}{s}" for t in range(NT) for s in range(2)] + [f"kt{t}" for t in range(NT)] + ["sc"]
    jobs += [f"m{n}" for n in range(2 * NB)] + [f"b1{n}" for n in range(NB)]
    jobs += ["od0", "od1"] + [f"ot{n}" for n in range(NB)] + [f"b0{n}" for n in range(NB)]
    jobs += [f"wo{n}" for n in range(NB)] + [f"yt{t}{s}" for t in range(NT) for s in range(2)]
    jobs += [f"xt{n}" for n in range(NB)] + ["lg", "rk", "wt", "bd0", "bd1", "bd2", "bd3", "bd4", "bd5", "bd6", "bd7"]
    return jobs


def build(nc, xT, w_in, w_branch, w_o, gla_w_a2, rg_w_a, rg_w_x, state_gla, pack, b_gu, ln1_g, ln1_b, ln2_g, ln2_b,
          router_b, w_gu, w_down, b_down, y_prompt, y_sample, gla_prompt, gla_sample, small):
    jobs = mixer_jobs()
    job = {n: i for i, n in enumerate(jobs)}

    q0, k0, v0, g0 = 0, H * DK, 2 * H * DK, 2 * H * DK + D
    low0 = g0 + D
    xr0 = low0 + RANK
    m0 = xr0 + D
    tiles = []

    def add_tiles(name, matrix, col, blocks):
        for b in range(0, blocks, 2):
            tiles.append((name, b, matrix, col + b * P))

    add_tiles("xr", w_in[0], xr0, NB)
    add_tiles("k", w_in[0], k0, H)
    add_tiles("q", w_in[0], q0, H)
    add_tiles("v", w_in[0], v0, NB)
    add_tiles("g", w_in[0], g0, NB)
    add_tiles("m", w_in[0], m0, 2 * NB)
    add_tiles("b1", w_branch[0, 1], 0, NB)
    add_tiles("b0", w_branch[0, 0], 0, NB)
    add_tiles("wo", w_o[0], 0, NB)
    tile_of = {f"{n}{b + j}": (i, j) for i, (n, b, _, _) in enumerate(tiles) for j in range(2)}

    with ExitStack() as ctx:
        def sb(name, shape, dt=F32):
            return ctx.enter_context(nc.sbuf_tensor(name, shape, dt))

        def ps(name, shape):
            return ctx.enter_context(nc.psum_tensor(name, shape, F32))

        def sem(name):
            return ctx.enter_context(nc.semaphore(name))

        gu_w = sb("gu_w", [P, NB, 2 * F])
        dn_w = sb("dn_w", [P, NB, D])
        ring = dn_w[:, :, :].rearrange("p (s a) n -> p s (a n)", a=2).rearrange("p s (k n) -> p s k n", n=WCOL)
        gate_w = gu_w[:, 7, :].rearrange("p (w n d) -> p w n d", w=2, n=NB)
        dstate = [gu_w[:, 5 + i // 2, (i % 2) * D:(i % 2 + 1) * D] for i in range(4)]
        x_in = sb("x_in", [P, NB, T])
        arena = sb("arena", [P, 10 * SLOT])

        def slot(i, first=0, size=SLOT):
            return arena[:, i * SLOT + first:i * SLOT + first + size]

        def blocks(ap, n):
            return ap.rearrange("p (n t) -> p n t", n=n)

        HALF = H * T
        cin = blocks(slot(0, 0, NB * CIN), NB)
        xc = blocks(slot(2), NB)
        rgate = blocks(slot(3), NB)
        igate = blocks(slot(4), NB)
        decay = blocks(slot(5), NB)
        root = blocks(slot(6), NB)
        ctmp = slot(6, 0, 2 * COUT).rearrange("p (a n) -> p a n", a=2)
        hs = blocks(slot(7), NB)
        kT = blocks(slot(8, 0, HALF), H)
        qT = blocks(slot(8, HALF, HALF), H)
        vT = blocks(slot(9), NB)
        za = blocks(slot(2, 0, HALF), H)
        zb = blocks(slot(2, HALF, HALF), H)
        bc = blocks(slot(3, 0, HALF), H)
        eb = blocks(slot(3, HALF, HALF), H)
        enb = blocks(slot(5, 0, HALF), H)
        kd = blocks(slot(5, HALF, HALF), H)
        qe = blocks(slot(4, 0, HALF), H)
        ke = blocks(slot(4, HALF, HALF), H)
        gT = blocks(slot(6), NB)
        vtok = slot(0, 0, NT * D).rearrange("p (t n) -> p t n", t=NT)
        kdt = slot(2, 0, NT * H * DK).rearrange("p (t n) -> p t n", t=NT)
        scs = slot(2, NT * H * DK, 8 * CH).rearrange("p (g t) -> p g t", t=CH)
        otok = slot(8, 0, NT * D).rearrange("p (t n) -> p t n", t=NT)
        mgla = blocks(slot(3), NB)
        mrg = blocks(slot(5), NB)
        oT = blocks(slot(4), NB)
        merged = blocks(slot(2), NB)
        yT = blocks(slot(0), NB)
        ytok = slot(8, 0, NT * D).rearrange("p (t n) -> p t n", t=NT)
        x1 = slot(5, 0, NT * D).rearrange("p (t n) -> p t n", t=NT)
        x1T = blocks(slot(4), NB)
        ln1 = slot(7, 0, 2 * D).rearrange("p (a n) -> p a n", a=2)
        ln2 = slot(3, 0, 2 * D).rearrange("p (a n) -> p a n", a=2)
        yacc = blocks(slot(4), NB)
        xg = blocks(slot(2, 0, NB * 2 * CAP), NB)
        HF = F // 2
        eo = slot(7, 0, 2 * HF).rearrange("p (j n) -> p j n", j=2)
        wpick = slot(7, D, NT * 4 * CAP).rearrange("p (t j d c) -> p t j d c", t=NT, j=2, d=2)
        gbuf, ubuf, tbuf, sbuf_ = (slot(8, i * HF, HF) for i in range(4))
        act_s = slot(9, 0, HF)
        act_t = slot(9, HF, HF).rearrange("p (c s) -> p c s", c=4)
        swT = slot(9, 2 * HF, 2 * T).rearrange("p (j t) -> p j t", j=2)
        pick = slot(9, 2 * HF + 2 * T, NT * 2 * CAP).rearrange("p (t c) -> p t c", t=NT)
        b3 = slot(1, 1024, F).bitcast(BF16)[0:3 * E, :]
        braw = gu_w[0:3 * E, 4, :]
        y2 = slot(0, 0, NT * D).rearrange("p (t n) -> p t n", t=NT)

        consts = sb("consts", [P, NPACK])

        def con(name):
            a, w = PACK[name]
            return consts[:, a:a + w]

        conv_w, conv_b = blocks(con("conv_w"), NB), con("conv_b")
        router_w = blocks(con("router_w"), NB)
        ident = sb("ident", [P, P])
        before = sb("before", [P, P])
        ones = sb("ones", [P, P])
        causal = sb("causal", [P, CH])
        keep = sb("keep", [P, T])
        iota = sb("iota", [P, CAP])
        low_w = sb("low_w", [P, NB, RANK])
        a2 = sb("a2", [RANK, H * DK])
        lowT = sb("lowT", [RANK, T])
        rb = sb("rb", [P, E])
        Sg = sb("Sg", [P, H, DV])
        bdn = Sg[:, :, :].rearrange("p h v -> p (h v)")
        km = slot(9, 1088, 2 * H * DK)[0:DEC, :].rearrange("p (a n) -> p a n", a=2)
        ebl = sb("ebl", [P, H, NCH])
        ebd = sb("ebd", [P, H, DEC])
        qd = sb("qd", [P, H, DEC])
        odT = sb("odT", [P, NB, DEC])
        sp_ = sb("sp_", [P, 5, NB])
        st = sb("st", [P, NT, H, 6])
        mv = sb("mv", [P, NT, H, 2])
        rs = sb("rs", [P, 2, NT * H])
        st1 = sb("st1", [P, NT, 2, 6])
        mv1 = sb("mv1", [P, NT, 2])
        rs1 = sb("rs1", [P, 2, NT])
        outs = sb("outs", [P, NOUT])
        lg = sb("lg", [P, NT, E])
        mx = sb("mx", [P, NT, 8])
        eq = sb("eq", [P, NT, E])
        cum = sb("cum", [P, NT, E])
        sel = sb("sel", [P, NT, E])
        ex = sb("ex", [P, NT, E])
        red = sb("red", [P, 4, NT])
        flag = sb("flag", [P, 1], I32)
        NRX = (PASSES + 1) * E
        x_flat = x_in[:, :, :].rearrange("p n t -> p (n t)")
        rankx = x_flat[:, 0:NT * NRX].rearrange("p (t e) -> p t e", t=NT)
        wtx = x_flat[:, NT * NRX:2 * NT * NRX].rearrange("p (t e) -> p t e", t=NT)
        which = sb("which", [3 * E, CAP])
        eid = sb("eid", [3 * E, E + 1])
        oh = sb("oh", [3 * E, CAP], BF16)
        wT = sb("wT", [E, T])

        pool4 = ps("pool4", [P, 4, 512])
        ub = ps("ub", [P, 2, 512])
        ob = ps("ob", [P, 2, 512])
        GATE, UP, DOWN, ACTT = (pool4[:, i, :] for i in range(4))
        SCAT2 = pool4[:, 2:4, :]
        GATH, SCAT = ub, ob

        tile_in = [sem(f"tile_in{i}") for i in range(4)]
        filled = [sem(f"filled{i}") for i in range(4)]
        drained = [sem(f"drained{i}") for i in range(4)]
        x_landed, pack_in, low_in, a2_in, gate_in = (sem(n) for n in ("x_landed", "pack_in", "low_in", "a2_in", "gate_in"))
        ln_in, ln2_in, rb_in, bdn_in = (sem(n) for n in ("ln_in", "ln2_in", "rb_in", "bdn_in"))
        dst_in = [sem(f"dst_in{i}") for i in range(4)]
        dst_out = [sem(f"dst_out{i}") for i in range(4)]
        stored = sem("stored")
        stored_early = sem("stored_early")
        pool_c = sem("pool_c")
        dve = sem("dve_step")
        act = sem("act_step")
        conv_done, rg_exp, rg_root, rg_rooted, rg_done = (sem(n) for n in ("conv_done", "rg_exp", "rg_root", "rg_rooted", "rg_done"))
        z_abs, z_min, z_ln, b_done, b_exp, gla_in = (sem(n) for n in ("z_abs", "z_min", "z_ln", "b_done", "b_exp", "gla_in"))
        gsig = sem("gsig")
        o_full, o_read, u_full, s_done = (sem(n) for n in ("o_full", "o_read", "u_full", "s_done"))
        km_done, d_full, d_done, od_full, od_sb = (sem(n) for n in ("km_done", "d_full", "d_done", "od_full", "od_sb"))
        o_var, o_std, o_norm = (sem(n) for n in ("o_var", "o_std", "o_norm"))
        y_var, y_std, y_norm, x1_done = (sem(n) for n in ("y_var", "y_std", "y_norm", "x1_done"))
        lg_done, ex_done, sel_done, wt_done, flag_done = (sem(n) for n in ("lg_done", "ex_done", "sel_done", "wt_done", "flag_done"))
        small_done = sem("small_done")
        gu_in = [sem(f"gu_in{k}") for k in range(NB)]
        dn_in = [sem(f"dn_in{k}") for k in range(NB)]
        gu_used, dn_used = sem("gu_used"), sem("dn_used")
        braw_in, b3_step, oh_ready = sem("braw_in"), sem("b3_step"), sem("oh_ready")
        act_tr, actt_ready = sem("act_tr"), sem("actt_ready")
        picked, wpicked = sem("picked"), sem("wpicked")
        gath_done, xg_ready = sem("gath_done"), sem("xg_ready")
        gu_read, gclip, sig_done, act_ready = (sem(n) for n in ("gu_read", "gclip", "sig_done", "act_ready"))
        eo_ready, scat_done, scat_read = (sem(n) for n in ("eo_ready", "scat_done", "scat_read"))
        moe_done, fin_full, fin_read, y2_var, y2_std, y2_norm, y2_done, tail = (
            sem(n) for n in ("moe_done", "fin_full", "fin_read", "y2_var", "y2_std", "y2_norm", "y2_done", "tail_step"))

        def bank(name):
            return pool4[:, job[name] % 4, :]

        def open_job(eng, name):
            i = job[name]
            if i >= 4:
                eng.wait_ge(drained[i % 4], i // 4)

        def wait_filled(eng, name):
            eng.wait_ge(filled[job[name] % 4], job[name] // 4 + 1)

        def wait_drained(eng, name):
            eng.wait_ge(drained[job[name] % 4], job[name] // 4 + 1)

        fl = lambda name: filled[job[name] % 4]
        dr = lambda name: drained[job[name] % 4]

        class Steps:
            def __init__(self, eng, s):
                self.eng, self.s, self.n, self.base = eng, s, 0, 0

            def done(self, ins):
                ins.then_inc(self.s, 1)
                self.n += 1

            def settle(self):
                self.eng.wait_ge(self.s, self.base + self.n)

        def moe_loops(eng, body):
            with eng.Fori(0, PAIRS) as pair:
                body(pair, pair)
            eng.wait_ge(flag_done, 1)
            over = eng.value_load(flag[0:1, 0:1], min_val=0, max_val=1)
            with eng.If(over == 1):
                with eng.Fori(1, PASSES) as turn:
                    with eng.Fori(0, PAIRS) as pair:
                        body(turn * PAIRS + pair, pair)

        block = ctx.enter_context(nc.Block())

        @block.sync
        def _(sp):
            sp.dma_start(x_in[:, :, :], xT).then_inc(x_landed, 16)
            for i, (name, b, matrix, col) in enumerate(tiles):
                if i >= 4:
                    former = tiles[i - 4]
                    wait_filled(sp, f"{former[0]}{former[1] + 1}")
                sp.dma_start(ring[:, i % 4, :, :],
                             matrix[:, col:col + WCOL].rearrange("(k p) n -> p k n", p=P)).then_inc(tile_in[i % 4], 16)
                if i == 0:
                    sp.dma_start(consts[:, :], pack).then_inc(pack_in, 16)
                    sp.dma_start(low_w[:, :, :], w_in[0, :, low0:low0 + RANK].rearrange("(k p) n -> p k n", p=P)
                                 ).then_inc(low_in, 16)
                    sp.dma_start(a2[:, :], gla_w_a2[0]).then_inc(a2_in, 16)
                if i == 2:
                    for part in range(3):
                        sp.dma_start(braw[part * E:(part + 1) * E, :], b_gu[0]).then_inc(braw_in, 16)
                if i == 1:
                    sp.dma_start(gate_w[:, 0, :, :], rg_w_a[0].rearrange("n c d -> c n d")).then_inc(gate_in, 16)
                    sp.dma_start(gate_w[:, 1, :, :], rg_w_x[0].rearrange("n c d -> c n d")).then_inc(gate_in, 16)
            sp.wait_ge(b3_step, 9)
            for i in range(4):
                sp.wait_ge(dst_out[i], 32)

            def body(it, pair):
                for j in range(2):
                    n = it * 2 + j
                    for k in range(NB):
                        sp.wait_ge(gu_used, n * NB + k + 1)
                        sp.dma_start(gu_w[:, k, :], w_gu[0, bass.ds(pair * 2 + j, 1), k * P:(k + 1) * P, :]
                                     .rearrange("e p n -> (e p) n")).then_inc(gu_in[k], 16)
                    for k in range(NB):
                        sp.wait_ge(dn_used, n * NB + k + 1)
                        sp.dma_start(dn_w[:, k, :], w_down[0, bass.ds(pair * 2 + j, 1), k * P:(k + 1) * P, :]
                                     .rearrange("e p n -> (e p) n")).then_inc(dn_in[k], 16)

            moe_loops(sp, body)
            for t, (first, rows) in enumerate(TILES):
                sp.wait_ge(y2_done, t + 1)
                dst = y_prompt[0, first:first + rows, :] if t < 2 else y_sample.rearrange("b s d -> (b s) d")
                sp.dma_start(dst, y2[0:rows, t, :]).then_inc(stored, 16)
            sp.wait_ge(stored, 16 * NT)

        @block.gpsimd
        def _(pool):
            g = nc.gpsimd
            g.memset(ident[:, :], 0.0).then_inc(pool_c, 1)
            g.memset(ones[:, :], 1.0).then_inc(pool_c, 1)
            g.memset(keep[:, :], 1.0).then_inc(pool_c, 1)
            g.iota(iota[:, :], pattern=[[1, CAP]], base=0, channel_multiplier=0,
                   allow_small_or_imprecise_dtypes=True).then_inc(pool_c, 1)
            pool.wait_ge(pool_c, 4)
            g.affine_select(out=ident[:, :], in_=ident[:, :], compare_op=ALU.not_equal, fill=1.0, base=0,
                            pattern=[[-1, P]], channel_multiplier=1).then_inc(pool_c, 1)
            g.affine_select(out=before[:, :], in_=ones[:, :], compare_op=ALU.is_gt, fill=0.0, base=0,
                            pattern=[[1, P]], channel_multiplier=-1).then_inc(pool_c, 1)
            for c in range(2):
                pool.wait_ge(pool_c, 6 + c)
                g.affine_select(out=causal[c * CH:(c + 1) * CH, :], in_=ones[c * CH:(c + 1) * CH, 0:CH],
                                compare_op=ALU.is_ge, fill=0.0, base=0, pattern=[[1, CH]],
                                channel_multiplier=-1).then_inc(pool_c, 1)
            pool.wait_ge(pool_c, 8)
            g.memset(keep[:, 0:SEQ:CH], 0.0).then_inc(pool_c, 1)
            g.memset(keep[:, SEQ:T], 0.0).then_inc(pool_c, 1)
            for part in range(3):
                pool.wait_ge(pool_c, 10 + part)
                g.iota(which[part * E:(part + 1) * E, :], pattern=[[0, CAP]], base=0, channel_multiplier=1,
                       allow_small_or_imprecise_dtypes=True).then_inc(pool_c, 1)
            pool.wait_ge(pool_c, 13)
            g.iota(eid[:, 0:E], pattern=[[1, E]], base=0, channel_multiplier=0,
                   allow_small_or_imprecise_dtypes=True).then_inc(pool_c, 1)
            pool.wait_ge(pool_c, 14)
            g.memset(eid[:, E:E + 1], 0.0).then_inc(pool_c, 1)
            pool.wait_ge(braw_in, 48)
            n = 0
            for part in range(3):
                r = slice(part * E, (part + 1) * E)
                for _ in range(part):
                    pool.wait_ge(b3_step, n) if n else None
                    g.tensor_copy(b3[r, :], braw[r, :]).then_inc(b3_step, 1)
                    pool.wait_ge(b3_step, n + 1)
                    g.tensor_tensor(braw[r, :], braw[r, :], b3[r, :], ALU.subtract).then_inc(b3_step, 1)
                    n += 2
                if n:
                    pool.wait_ge(b3_step, n)
                g.tensor_copy(b3[r, :], braw[r, :]).then_inc(b3_step, 1)
                n += 1
            for b in range(DEC):
                i = b % 4
                if b >= 4:
                    pool.wait_ge(d_done, b - 3)
                    pool.wait_ge(od_full, b - 3)
                    pool.dma_start(gla_sample[0, b - 4].rearrange("h p v -> p h v"),
                                   dstate[i].rearrange("p (h v) -> p h v", h=H)).then_inc(dst_out[i], 16)
                    pool.wait_ge(dst_out[i], 16)
                pool.dma_start(dstate[i].rearrange("p (h v) -> p h v", h=H),
                               state_gla[0, b].rearrange("h p v -> p h v")).then_inc(dst_in[i], 16)
                if b == 3:
                    pool.dma_start(rb[:, :], router_b.partition_broadcast(P).rearrange("p a e -> p (a e)")).then_inc(rb_in, 16)
            for b in range(4, DEC):
                pool.wait_ge(d_done, b + 1)
                pool.wait_ge(od_full, b + 1)
                pool.dma_start(gla_sample[0, b].rearrange("h p v -> p h v"),
                               dstate[b % 4].rearrange("p (h v) -> p h v", h=H)).then_inc(dst_out[b % 4], 16)
            pool.wait_ge(s_done, NCH * H)
            pool.dma_start(gla_prompt[0, 0].rearrange("h p v -> p h v"), Sg[:, :, :]).then_inc(stored_early, 16)
            pool.wait_ge(small_done, 4)
            pool.dma_start(small, outs[:, :]).then_inc(stored_early, 16)
            pool.wait_ge(stored_early, 32)
            pool.dma_start(bdn[0:E, :], b_down[0]).then_inc(bdn_in, 16)
            wait_filled(pool, "b17")
            wait_filled(pool, "b16")
            pool.dma_start(ln1[:, 0, :], ln1_g.partition_broadcast(P).rearrange("p a e -> p (a e)")).then_inc(ln_in, 16)
            pool.dma_start(ln1[:, 1, :], ln1_b.partition_broadcast(P).rearrange("p a e -> p (a e)")).then_inc(ln_in, 16)
            wait_drained(pool, "b07")
            pool.dma_start(ln2[:, 0, :], ln2_g.partition_broadcast(P).rearrange("p a e -> p (a e)")).then_inc(ln2_in, 16)
            pool.dma_start(ln2[:, 1, :], ln2_b.partition_broadcast(P).rearrange("p a e -> p (a e)")).then_inc(ln2_in, 16)
            for i in range(4):
                pool.wait_ge(dst_out[i], 32)

        @block.tensor
        def _(pe):
            mm = nc.tensor.matmul

            def project(name, rhs):
                i, half = tile_of[name]
                pe.wait_ge(tile_in[i % 4], 16 * (i // 4 + 1))
                open_job(pe, name)
                for k in range(NB):
                    last = mm(bank(name)[:, 0:T], ring[:, i % 4, k, half * P:(half + 1) * P], rhs[:, k, :],
                              start=(k == 0), stop=(k == NB - 1))
                last.then_inc(fl(name), 1)

            def turn(name, pieces):
                open_job(pe, name)
                for out, in_ in pieces:
                    rows = in_.shape[0]
                    last = nc.tensor.transpose(out, in_, ident[0:rows, 0:rows])
                last.then_inc(fl(name), 1)

            pe.wait_ge(x_landed, 16)
            for n in range(NB):
                project(f"xr{n}", x_in)
            open_job(pe, "low")
            pe.wait_ge(low_in, 16)
            for k in range(NB):
                last = mm(bank("low")[0:RANK, 0:T], low_w[:, k, :], x_in[:, k, :], start=(k == 0), stop=(k == NB - 1))
            last.then_inc(fl("low"), 1)
            for n in range(H):
                project(f"k{n}", x_in)
            pe.wait_ge(gate_in, 32)
            for n in range(NB):
                pe.wait_ge(conv_done, n + 1)
                for w, name in enumerate((f"r{n}", f"i{n}")):
                    open_job(pe, name)
                    mm(bank(name)[:, 0:T], gate_w[:, w, n, :], xc[:, n, :], start=True, stop=True).then_inc(fl(name), 1)
            for n in range(H):
                project(f"q{n}", x_in)
            for n in range(NB):
                project(f"v{n}", x_in)
            wait_drained(pe, "low")
            pe.wait_ge(a2_in, 16)
            for h in range(H):
                open_job(pe, f"z{h}")
                mm(bank(f"z{h}")[:, 0:T], a2[:, h * DK:(h + 1) * DK], lowT[:, :], start=True, stop=True
                   ).then_inc(fl(f"z{h}"), 1)
            for n in range(NB):
                project(f"g{n}", x_in)
            pe.wait_ge(pool_c, 10)
            for n in range(NB):
                wait_drained(pe, f"v{n}")
            for t, (first, rows) in enumerate(TILES):
                for s in range(2):
                    name = f"vt{t}{s}"
                    turn(name, [(bank(name)[0:rows, c * P:(c + 1) * P], vT[:, 4 * s + c, first:first + rows])
                                for c in range(4)])
            pe.wait_ge(gla_in, 4)
            for t, (first, rows) in enumerate(TILES):
                name = f"kt{t}"
                turn(name, [(bank(name)[0:rows, h * DK:(h + 1) * DK], kd[:, h, first:first + rows]) for h in range(H)])
            open_job(pe, "sc")
            for c in range(NCH):
                p0, cols = (c % 2) * CH, slice(c * CH, (c + 1) * CH)
                for h in range(H):
                    g = 2 * h + c // 2
                    last = mm(bank("sc")[p0:p0 + CH, g * CH:(g + 1) * CH], ke[:, h, cols], qe[:, h, cols],
                              start=True, stop=True)
            last.then_inc(fl("sc"), 1)

            def chunk(c):
                t, p0, cols = c // 2, (c % 2) * CH, slice(c * CH, (c + 1) * CH)
                rows = slice(p0, p0 + CH)
                if c == 2:
                    pe.wait_ge(o_read, 1)
                for h in range(H):
                    out = ob[rows, h // 2, (h % 2) * DV:(h % 2 + 1) * DV]
                    if c:
                        pe.wait_ge(s_done, (c - 1) * H + h + 1)
                    last = mm(out, scs[rows, 2 * h + t, :], vtok[rows, t, h * DV:(h + 1) * DV],
                              start=True, stop=(c == 0))
                    if c:
                        last = mm(out, qe[:, h, cols], Sg[:, h, :], start=False, stop=True)
                last.then_inc(o_full, 1)
                for h in range(H):
                    if c and h % 2 == 0:
                        pe.wait_ge(s_done, (c - 1) * H + h + 2)
                    last = mm(ub[:, h // 2, (h % 2) * DV:(h % 2 + 1) * DV], kdt[rows, t, h * DK:(h + 1) * DK],
                              vtok[rows, t, h * DV:(h + 1) * DV], start=True, stop=True)
                    if h % 2:
                        last.then_inc(u_full, 1)

            for name in [f"vt{t}{s}" for t in range(NT) for s in range(2)] + [f"kt{t}" for t in range(NT)] + ["sc"]:
                wait_drained(pe, name)
            for c in range(NCH):
                chunk(c)
                project(f"m{2 * c}", x_in)
                project(f"m{2 * c + 1}", x_in)
            pe.wait_ge(o_read, 2)
            for b in range(DEC):
                pe.wait_ge(km_done, b + 1)
                pe.wait_ge(s_done, NCH * H)
                if b:
                    pe.wait_ge(d_done, b)
                for h in range(H):
                    last = mm(ub[:, h // 2, (h % 2) * DV:(h % 2 + 1) * DV], km[:, b % 2, h * DK:(h + 1) * DK],
                              vtok[0:DEC, 2, h * DV:(h + 1) * DV], start=True, stop=True)
                last.then_inc(d_full, 1)
                project(f"m{NB + b}", x_in)
                pe.wait_ge(d_done, b + 1)
                for n in range(NB):
                    h, col = n // 2, (n % 2) * P
                    last = mm(ob[:, 0, n * DEC + b:n * DEC + b + 1],
                              dstate[b % 4][:, h * DV + col:h * DV + col + P], qd[:, h, b:b + 1],
                              start=(b == 0 and n == 0), stop=True, skip_group_check=True)
                last.then_inc(od_full, 1)
            pe.wait_ge(od_full, DEC)
            pe.sem_inc(gu_used, NB)
            pe.wait_ge(rg_done, 2)
            for n in range(NB):
                project(f"b1{n}", hs)
            pe.wait_ge(od_sb, 1)
            for s in range(2):
                name = f"od{s}"
                turn(name, [(bank(name)[0:DEC, c * P:(c + 1) * P], odT[:, 4 * s + c, :]) for c in range(4)])
            pe.wait_ge(o_norm, NT)
            for n in range(NB):
                name = f"ot{n}"
                turn(name, [(bank(name)[:, first:first + rows], otok[0:rows, t, n * P:(n + 1) * P])
                            for t, (first, rows) in enumerate(TILES)])
            for n in range(NB):
                wait_drained(pe, f"ot{n}")
            for n in range(NB):
                project(f"b0{n}", oT)
            for n in range(NB):
                wait_drained(pe, f"b0{n}")
            for n in range(NB):
                project(f"wo{n}", merged)
            wait_filled(pe, "wo7")
            pe.sem_inc(dn_used, NB)
            for n in range(NB):
                wait_drained(pe, f"wo{n}")
            for t, (first, rows) in enumerate(TILES):
                for s in range(2):
                    name = f"yt{t}{s}"
                    turn(name, [(bank(name)[0:rows, c * P:(c + 1) * P], yT[:, 4 * s + c, first:first + rows])
                                for c in range(4)])
            pe.wait_ge(y_norm, NT)
            for n in range(NB):
                name = f"xt{n}"
                turn(name, [(bank(name)[:, first:first + rows], ytok[0:rows, t, n * P:(n + 1) * P])
                            for t, (first, rows) in enumerate(TILES)])
            for n in range(NB):
                wait_drained(pe, f"xt{n}")
            open_job(pe, "lg")
            for t, (first, rows) in enumerate(TILES):
                for k in range(NB):
                    last = mm(bank("lg")[0:rows, t * E:(t + 1) * E], x1T[:, k, first:first + rows], router_w[:, k, :],
                              start=(k == 0), stop=(k == NB - 1))
            last.then_inc(fl("lg"), 1)
            pe.wait_ge(sel_done, 1)
            open_job(pe, "rk")
            for t in range(NT):
                for s in range(t + 1):
                    mm(bank("rk")[:, t * E:(t + 1) * E], (before if s == t else ones)[:, :], sel[:, s, :],
                       start=(s == 0), stop=(s == t))
            for s in range(NT):
                last = mm(bank("rk")[:, NT * E:(NT + 1) * E], ones[:, :], sel[:, s, :], start=(s == 0), stop=(s == NT - 1))
            last.then_inc(fl("rk"), 1)
            pe.wait_ge(wt_done, 1)
            turn("wt", [(bank("wt")[0:E, first:first + rows], wtx[0:rows, t, 0:E]) for t, (first, rows) in enumerate(TILES)])
            wait_drained(pe, "wt")
            pe.wait_ge(bdn_in, 16)
            for n in range(NB):
                name = f"bd{n}"
                open_job(pe, name)
                mm(bank(name)[:, 0:T], bdn[0:E, n * P:(n + 1) * P], wT[:, :], start=True, stop=True
                   ).then_inc(fl(name), 1)

            def gather(j):
                for c in range(4):
                    n = 4 * j + c
                    for t, (first, rows) in enumerate(TILES):
                        last = mm(GATH[:, j, c * P:(c + 1) * P], x1[0:rows, t, n * P:(n + 1) * P],
                                  pick[0:rows, t, :], start=(t == 0), stop=(t == NT - 1))
                last.then_inc(gath_done, 1)

            pe.wait_ge(x1_done, NT)
            pe.wait_ge(picked, 1)
            gather(0)
            gather(1)
            for n in range(NB):
                wait_drained(pe, f"bd{n}")

            def body(it, pair):
                for j in range(2):
                    n = it * 2 + j
                    if j == 0:
                        pe.wait_ge(xg_ready, it + 1)
                    pe.wait_ge(gu_read, n + 1)
                    pe.wait_ge(oh_ready, n + 1)
                    quarters = [((GATE, UP)[f // 2][f % 2 * CAP:(f % 2 + 1) * CAP, :], slice(f * HF, (f + 1) * HF))
                                for f in range(4)]
                    for out, cols in quarters:
                        mm(out, oh[:, :], b3[:, cols], start=True, stop=False)
                    for k in range(NB):
                        pe.wait_ge(gu_in[k], n * 16 + 16)
                        for out, cols in quarters:
                            last = mm(out, xg[:, k, j * CAP:(j + 1) * CAP], gu_w[:, k, cols],
                                      start=False, stop=(k == NB - 1))
                        last.then_inc(gu_used, 1)
                    if j == 0:
                        pe.wait_ge(wpicked, it + 1)
                        pe.wait_ge(scat_read, it * 5 + 1)
                        for x in range(2):
                            for t, (first, rows) in enumerate(TILES):
                                last = nc.tensor.transpose(SCAT[:, x, first:first + rows],
                                                           wpick[0:rows, t, x, :, :].rearrange("p d c -> p (d c)"),
                                                           ident[0:rows, 0:rows])
                        last.then_inc(scat_done, 1)
                        pe.wait_ge(picked, it + 2)
                    gather(j)
                    pe.wait_ge(act_ready, n + 1)
                    for c in range(4):
                        last = nc.tensor.transpose(ACTT[:, c * P:(c + 1) * P], act_s[:, c * P:(c + 1) * P], ident[:, :])
                    last.then_inc(act_tr, 1)
                    pe.wait_ge(actt_ready, n + 1)
                    pe.wait_ge(eo_ready, n + 1)
                    for k in range(NB):
                        pe.wait_ge(dn_in[k], n * 16 + 16)
                        for s in range(2):
                            last = mm(DOWN[s * CAP:(s + 1) * CAP, :], act_t[:, k % 4, k // 4 * CAP:(k // 4 + 1) * CAP],
                                      dn_w[:, k, s * HF:(s + 1) * HF], start=(k == 0), stop=(k == NB - 1))
                        last.then_inc(dn_used, 1)
                pe.wait_ge(eo_ready, it * 2 + 3)
                for d in range(4):
                    pe.wait_ge(scat_read, it * 5 + 2 + max(d - 1, 0))
                    banks = SCAT if d % 2 == 0 else SCAT2
                    for x in range(2):
                        for s in range(2):
                            r = slice(s * CAP, (s + 1) * CAP)
                            last = mm(banks[:, s, 0:T], eo[r, x, d * P:(d + 1) * P], swT[r, x, :],
                                      start=(x == 0), stop=(x == 1))
                    last.then_inc(scat_done, 1)

            moe_loops(pe, body)
            pe.wait_ge(moe_done, 1)
            u = 0
            for t, (first, rows) in enumerate(TILES):
                for s in range(2):
                    if u >= 2:
                        pe.wait_ge(fin_read, u - 1)
                    for c in range(4):
                        last = nc.tensor.transpose(pool4[0:rows, u % 2, c * P:(c + 1) * P],
                                                   yacc[:, 4 * s + c, first:first + rows], ident[:, :])
                    last.then_inc(fin_full, 1)
                    u += 1

        @block.scalar
        def _(sc):
            me = Steps(sc, act)
            a = nc.scalar.activation
            sc.wait_ge(pack_in, 16)
            me.done(a(sp_[:, 0, :], con("lam"), ACT.Abs))
            me.settle()
            me.done(a(sp_[:, 0, :], sp_[:, 0, :], ACT.Exp, scale=-1.0))
            me.settle()
            a(sp_[:, 1, :], sp_[:, 0, :], ACT.Ln, bias=1.0).then_inc(z_ln, 1)
            for n in range(NB):
                wait_filled(sc, f"xr{n}")
                nc.scalar.copy(cin[:, n, CW - 1:CW - 1 + SEQ], bank(f"xr{n}")[:, 0:SEQ])
                nc.scalar.copy(cin[:, n, 2 * (CW - 1) + SEQ:CIN:CW], bank(f"xr{n}")[:, SEQ:T]).then_inc(dr(f"xr{n}"), 1)
            wait_filled(sc, "low")
            nc.scalar.copy(lowT[:, :], bank("low")[0:RANK, 0:T]).then_inc(dr("low"), 1)
            for h in range(H):
                wait_filled(sc, f"k{h}")
                nc.scalar.copy(kT[:, h, :], bank(f"k{h}")[:, 0:T]).then_inc(dr(f"k{h}"), 1)
            for n in range(NB):
                for name, dst, bias in ((f"r{n}", rgate, "b_r"), (f"i{n}", igate, "b_i")):
                    wait_filled(sc, name)
                    a(dst[:, n, :], bank(name)[:, 0:T], ACT.Sigmoid, bias=con(bias)[:, n:n + 1]).then_inc(dr(name), 1)
            for h in range(H):
                wait_filled(sc, f"q{h}")
                nc.scalar.mul(qT[:, h, :], bank(f"q{h}")[:, 0:T], DK ** -0.5).then_inc(dr(f"q{h}"), 1)
            sc.wait_ge(z_min, 1)
            for n in range(NB):
                wait_drained(sc, f"r{n}")
            for n in range(NB):
                a(decay[:, n, :], rgate[:, n, :], ACT.Exp, scale=sp_[:, 3, n:n + 1]).then_inc(rg_exp, 1)
            for n in range(NB):
                a(rgate[:, n, :], rgate[:, n, :], ACT.Tanh, scale=sp_[:, 4, n:n + 1]).then_inc(rg_exp, 1)
            for n in range(4):
                wait_filled(sc, f"v{n}")
                nc.scalar.copy(vT[:, n, :], bank(f"v{n}")[:, 0:T]).then_inc(dr(f"v{n}"), 1)
            sc.wait_ge(rg_root, 1)
            a(root, root, ACT.Sqrt).then_inc(rg_rooted, 1)
            for n in range(4, NB):
                wait_filled(sc, f"v{n}")
                nc.scalar.copy(vT[:, n, :], bank(f"v{n}")[:, 0:T]).then_inc(dr(f"v{n}"), 1)
            sc.wait_ge(rg_done, 2)
            for h in range(H):
                wait_filled(sc, f"z{h}")
                a(zb[:, h, :], bank(f"z{h}")[:, 0:T], ACT.Abs, bias=con("b_a")[:, h:h + 1]).then_inc(z_abs, 1)
            sc.wait_ge(z_abs, H)
            me.done(a(zb, zb, ACT.Exp, scale=-1.0))
            me.settle()
            a(zb, zb, ACT.Ln, bias=1.0).then_inc(z_ln, 1)
            sc.wait_ge(b_done, 1)
            a(eb, bc, ACT.Exp, scale=1.0 / 16).then_inc(b_exp, 1)
            a(enb, bc, ACT.Exp, scale=-1.0 / 16).then_inc(b_exp, 1)
            sc.wait_ge(b_done, 2)
            a(zb[:, :, 0:SEQ], zb[:, :, 0:SEQ], ACT.Exp, scale=-1.0 / 16).then_inc(b_exp, 1)
            for n in range(NB):
                wait_filled(sc, f"g{n}")
                a(gT[:, n, :], bank(f"g{n}")[:, 0:T], ACT.Sigmoid).then_inc(gsig, 1)
            for t, (first, rows) in enumerate(TILES):
                for s in range(2):
                    name = f"vt{t}{s}"
                    wait_filled(sc, name)
                    nc.scalar.copy(vtok[0:rows, t, s * 512:(s + 1) * 512], bank(name)[0:rows, :]).then_inc(dr(name), 1)

            def merge_gate(n):
                wait_filled(sc, f"m{n}")
                dst = mgla[:, n, :] if n < NB else mrg[:, n - NB, :]
                a(dst, bank(f"m{n}")[:, 0:T], ACT.Sigmoid, bias=con("b_merge")[:, n:n + 1]).then_inc(dr(f"m{n}"), 1)

            sc.wait_ge(gla_in, 5)
            for name in ("kt0", "kt1", "kt2"):
                wait_filled(sc, name)
            for c in range(NCH):
                if c % 2 == 1:
                    sc.wait_ge(o_full, c + 1)
                    nc.scalar.copy(otok[:, c // 2, :], ob[:, :, :].rearrange("p a n -> p (a n)")).then_inc(o_read, 1)
                merge_gate(2 * c)
                merge_gate(2 * c + 1)
            for b in range(DEC):
                merge_gate(NB + b)
            sc.wait_ge(od_full, DEC)
            nc.scalar.copy(odT[:, :, :].rearrange("p n b -> p (n b)"), ob[:, 0, 0:NB * DEC]).then_inc(od_sb, 1)
            sc.wait_ge(o_var, 1)
            a(rs[:, 0, 0:2 * H], rs[:, 0, 0:2 * H], ACT.Sqrt).then_inc(o_std, 1)
            for s in range(2):
                wait_filled(sc, f"od{s}")
                nc.scalar.copy(otok[0:DEC, 2, s * 512:(s + 1) * 512], bank(f"od{s}")[0:DEC, :]).then_inc(dr(f"od{s}"), 1)
            sc.wait_ge(o_var, 2)
            a(rs[0:DEC, 0, 2 * H:3 * H], rs[0:DEC, 0, 2 * H:3 * H], ACT.Sqrt).then_inc(o_std, 1)
            for n in range(NB):
                wait_filled(sc, f"ot{n}")
            for t, (first, rows) in enumerate(TILES):
                for s in range(2):
                    name = f"yt{t}{s}"
                    wait_filled(sc, name)
                    nc.scalar.copy(ytok[0:rows, t, s * 512:(s + 1) * 512], bank(name)[0:rows, :]).then_inc(dr(name), 1)
            for t, (first, rows) in enumerate(TILES):
                sc.wait_ge(y_var, t + 1)
                a(rs1[0:rows, 0, t:t + 1], rs1[0:rows, 0, t:t + 1], ACT.Sqrt).then_inc(y_std, 1)
            for n in range(NB):
                wait_filled(sc, f"xt{n}")
                a(x1T[:, n, :], bank(f"xt{n}")[:, 0:T], ACT.Identity, bias=con("ln1_b")[:, n:n + 1],
                  scale=con("ln1_g")[:, n:n + 1]).then_inc(dr(f"xt{n}"), 1)
            for t, (first, rows) in enumerate(TILES):
                sc.wait_ge(lg_done, t + 1)
                a(ex[0:rows, t, :], lg[0:rows, t, :], ACT.Exp, bias=red[0:rows, 0, t:t + 1]).then_inc(ex_done, 1)
            sc.wait_ge(gath_done, 2)
            nc.scalar.copy(xg, GATH[:, :, :].rearrange("p a n -> p (a n)").rearrange("p (n c) -> p n c", n=NB)
                           ).then_inc(xg_ready, 1)
            nc.scalar.copy(eo[0:1, 0, 0:1], ident[0:1, 0:1]).then_inc(eo_ready, 1)

            def body(it, pair):
                for j in range(2):
                    n = it * 2 + j
                    sc.wait_ge(gclip, n + 1)
                    a(sbuf_, gbuf, ACT.Sigmoid, scale=SWISH).then_inc(sig_done, 1)
                    sc.wait_ge(act_tr, n + 1)
                    nc.scalar.copy(act_t, ACTT.rearrange("p (c s) -> p c s", c=4)).then_inc(actt_ready, 1)
                    if j == 1:
                        sc.wait_ge(gath_done, it * 2 + 4)
                        nc.scalar.copy(xg, GATH[:, :, :].rearrange("p a n -> p (a n)").rearrange("p (n c) -> p n c", n=NB)
                                       ).then_inc(xg_ready, 1)
                    sc.wait_ge(dn_used, n * NB + 2 * NB)
                    sc.wait_ge(scat_done, it * 5 + 1)
                    nc.scalar.copy(eo[:, j, :], DOWN).then_inc(eo_ready, 1)

            moe_loops(sc, body)
            for t, (first, rows) in enumerate(TILES):
                sc.wait_ge(y2_var, t + 1)
                a(rs1[0:rows, 0, t:t + 1], rs1[0:rows, 0, t:t + 1], ACT.Sqrt).then_inc(y2_std, 1)

        @block.vector
        def _(v):
            me = Steps(v, dve)
            V = nc.vector
            stt, tt, ts = V.scalar_tensor_tensor, V.tensor_tensor, V.tensor_scalar
            me.done(V.memset(cin[:, :, 0:CW - 1], 0.0))
            v.wait_ge(pack_in, 16)
            me.done(V.tensor_copy(cin[:, :, CW - 1 + SEQ:CIN].rearrange("p n (b f) -> p n b f", f=CW)[:, :, :, 0:CW - 1],
                                  con("conv0").rearrange("p (n b f) -> p n b f", n=NB, b=DEC)))
            me.settle()
            me.done(ts(sp_[:, 2, :], con("lam"), -1.0, 0.0, ALU.mult, ALU.max))
            me.settle()
            v.wait_ge(z_ln, 1)
            me.done(tt(sp_[:, 2, :], sp_[:, 2, :], sp_[:, 1, :], ALU.add))
            me.settle()
            me.done(ts(sp_[:, 3, :], sp_[:, 2, :], -8.0, None, ALU.mult))
            ts(sp_[:, 4, :], sp_[:, 2, :], 8.0, None, ALU.mult).then_inc(z_min, 1)
            for n in range(NB):
                wait_drained(v, f"xr{n}")
                w = lambda j: conv_w[:, n, j:j + 1]
                tmp = ctmp[:, 0, :]
                me.settle()
                if n:
                    v.wait_ge(conv_done, n)
                me.done(ts(tmp, cin[:, n, 0:COUT], w(0), conv_b[:, n:n + 1], ALU.mult, ALU.add))
                me.settle()
                for j in range(1, CW - 1):
                    nxt = ctmp[:, j % 2, :]
                    me.done(stt(nxt, cin[:, n, j:j + COUT], w(j), tmp, ALU.mult, ALU.add))
                    me.settle()
                    tmp = nxt
                me.done(stt(xc[:, n, SEQ:T], cin[:, n, SEQ + 2 * (CW - 1):CIN:CW], w(CW - 1),
                            tmp[:, SEQ + CW - 1:COUT:CW], ALU.mult, ALU.add))
                stt(xc[:, n, 0:SEQ], cin[:, n, CW - 1:CW - 1 + SEQ], w(CW - 1), tmp[:, 0:SEQ], ALU.mult, ALU.add
                    ).then_inc(conv_done, 1)
            v.wait_ge(conv_done, NB)
            V.tensor_copy(outs[:, OUT_CONVP:OUT_CONVS].rearrange("p (n f) -> p n f", n=NB),
                          cin[:, :, SEQ:SEQ + CW - 1]).then_inc(small_done, 1)
            V.tensor_copy(outs[:, OUT_CONVS:OUT_HP].rearrange("p (n b f) -> p n b f", n=NB, b=DEC),
                          cin[:, :, CW - 1 + SEQ:CIN].rearrange("p n (b f) -> p n b f", f=CW)[:, :, :, 1:CW]
                          ).then_inc(small_done, 1)
            v.wait_ge(rg_exp, NB)
            me.done(tt(root, decay, decay, ALU.mult))
            me.settle()
            v.wait_ge(rg_exp, 2 * NB)
            stt(root, root, 1.0, rgate, ALU.add, ALU.mult).then_inc(rg_root, 1)
            for n in range(NB):
                wait_drained(v, f"i{n}")
            me.done(tt(igate, igate, xc, ALU.mult))
            me.settle()
            v.wait_ge(rg_rooted, 1)
            me.done(tt(igate, igate, root, ALU.mult))
            me.settle()
            h0 = blocks(con("h0"), NB)
            me.done(tt(hs[:, :, SEQ:T], decay[:, :, SEQ:T], h0, ALU.mult))
            me.settle()
            me.done(tt(hs[:, :, SEQ:T], hs[:, :, SEQ:T], igate[:, :, SEQ:T], ALU.add))
            for n in range(NB):
                me.done(V.tensor_tensor_scan(hs[:, n, 0:SEQ], decay[:, n, 0:SEQ], igate[:, n, 0:SEQ], 0.0,
                                             ALU.mult, ALU.add))
            me.settle()
            V.tensor_copy(outs[:, OUT_HP:OUT_HS].rearrange("p (n f) -> p n f", f=1), hs[:, :, SEQ - 1:SEQ]
                          ).then_inc(small_done, 1)
            V.tensor_copy(blocks(outs[:, OUT_HS:NOUT], NB), hs[:, :, SEQ:T]).then_inc(small_done, 1)
            v.wait_ge(small_done, 4)
            V.memset(mx[:, :, :], 0.0).then_inc(rg_done, 1)
            V.memset(lg[:, :, :], 0.0).then_inc(rg_done, 1)
            for h in range(H):
                v.wait_ge(z_abs, h + 1)
                ts(za[:, h, :], bank(f"z{h}")[:, 0:T], con("b_a")[:, h:h + 1], 0.0, ALU.add, ALU.min
                   ).then_inc(dr(f"z{h}"), 1)
            for h in range(H):
                wait_drained(v, f"z{h}")
            v.wait_ge(z_ln, 2)
            me.done(tt(za, za, zb, ALU.subtract))
            me.settle()
            v.wait_ge(pool_c, 10)
            for h in range(H):
                me.done(V.tensor_tensor_scan(bc[:, h, :], keep[:, :], za[:, h, :], 0.0, ALU.mult, ALU.add))
            me.settle()
            bcc = bc[:, :, 0:SEQ].rearrange("p h (c t) -> p h c t", c=NCH)
            V.tensor_copy(ebl[:, :, :], bcc[:, :, :, CH - 1]).then_inc(b_done, 1)
            v.wait_ge(b_done, 1)
            tt(zb[:, :, 0:SEQ].rearrange("p h (c t) -> p h c t", c=NCH), bcc,
               ebl[:, :, :].unsqueeze(3).to_broadcast([P, H, NCH, CH]), ALU.subtract).then_inc(b_done, 1)
            v.wait_ge(b_exp, 2)
            tt(qe, qT, eb, ALU.mult).then_inc(gla_in, 1)
            tt(ke, kT, enb, ALU.mult).then_inc(gla_in, 1)
            v.wait_ge(b_exp, 3)
            tt(kd[:, :, 0:SEQ], kT[:, :, 0:SEQ], zb[:, :, 0:SEQ], ALU.mult).then_inc(gla_in, 1)
            V.tensor_copy(kd[:, :, SEQ:T], kT[:, :, SEQ:T]).then_inc(gla_in, 1)
            v.wait_ge(b_done, 2)
            me.done(V.tensor_copy(ebl[:, :, :], eb[:, :, CH - 1:SEQ:CH]))
            me.done(V.tensor_copy(qd[:, :, :], qT[:, :, SEQ:T]))
            V.tensor_copy(ebd[:, :, :], eb[:, :, SEQ:T]).then_inc(gla_in, 1)
            for n in range(NB):
                v.wait_ge(gsig, n + 1)
                stt(gT[:, n, :], bank(f"g{n}")[:, 0:T], con("norm_g")[:, n:n + 1], gT[:, n, :], ALU.mult, ALU.mult
                    ).then_inc(dr(f"g{n}"), 1)
            for t, (first, rows) in enumerate(TILES):
                name = f"kt{t}"
                wait_filled(v, name)
                V.tensor_copy(kdt[0:rows, t, :], bank(name)[0:rows, :]).then_inc(dr(name), 1)
            wait_filled(v, "sc")
            tt(scs, bank("sc").rearrange("p (g t) -> p g t", t=CH),
               causal[:, :].unsqueeze(1).to_broadcast([P, 8, CH]), ALU.mult).then_inc(dr("sc"), 1)
            wait_drained(v, "kt2")

            def k_row(b):
                ts(km[:, b % 2, :], kdt[0:DEC, 2, :], ident[0:DEC, b:b + 1], None, ALU.mult).then_inc(km_done, 1)

            k_row(0)
            k_row(1)
            me.settle()
            v.wait_ge(gla_in, 5)
            for c in range(NCH):
                for h in range(H):
                    if h % 2 == 0:
                        v.wait_ge(u_full, c * 2 + h // 2 + 1)
                    if h == 0:
                        v.wait_ge(o_full, c + 1)
                        if c:
                            v.wait_ge(s_done, c * H)
                    u = ub[:, h // 2, (h % 2) * DV:(h % 2 + 1) * DV]
                    if c:
                        stt(Sg[:, h, :], Sg[:, h, :], ebl[:, h, c:c + 1], u, ALU.mult, ALU.add).then_inc(s_done, 1)
                    else:
                        V.tensor_copy(Sg[:, h, :], u).then_inc(s_done, 1)

            def norm_stats(tiles_):
                for t in tiles_:
                    rows = TILES[t][1]
                    for h in range(H):
                        me.done(V.bn_stats(st[0:rows, t, h, :], otok[0:rows, t, h * DV:(h + 1) * DV]))
                me.settle()
                for t in tiles_:
                    rows = TILES[t][1]
                    for h in range(H):
                        me.done(V.bn_aggr(mv[0:rows, t, h, :], st[0:rows, t, h, :]))
                me.settle()
                a, b, rows = tiles_[0], tiles_[-1] + 1, TILES[tiles_[0]][1]
                ts(rs[0:rows, 0, a * H:b * H].rearrange("p (t h) -> p t h", h=H), mv[0:rows, a:b, :, 1], EPS, None, ALU.add
                   ).then_inc(o_var, 1)

            for b in range(DEC):
                v.wait_ge(dst_in[b % 4], 16 * (b // 4 + 1))
                v.wait_ge(d_full, b + 1)
                for h in range(H):
                    sl = dstate[b % 4][:, h * DV:(h + 1) * DV]
                    last = stt(sl, sl, ebd[:, h, b:b + 1], ub[:, h // 2, (h % 2) * DV:(h % 2 + 1) * DV], ALU.mult, ALU.add)
                last.then_inc(d_done, 1)
                if b + 2 < DEC:
                    k_row(b + 2)
            v.wait_ge(o_read, 2)
            norm_stats([0, 1])

            def normalise(t):
                rows = TILES[t][1]
                for h in range(H):
                    o = otok[0:rows, t, h * DV:(h + 1) * DV]
                    last = ts(o, o, mv[0:rows, t, h, 0:1], rs[0:rows, 1, t * H + h:t * H + h + 1], ALU.subtract, ALU.mult)
                last.then_inc(o_norm, 1)

            v.wait_ge(o_std, 1)
            me.done(V.reciprocal(rs[:, 1, 0:2 * H], rs[:, 0, 0:2 * H]))
            me.settle()
            normalise(0)
            normalise(1)
            for n in range(NB):
                wait_filled(v, f"b1{n}")
                wait_drained(v, f"m{NB + n}")
                tt(merged[:, n, :], bank(f"b1{n}")[:, 0:T], mrg[:, n, :], ALU.mult).then_inc(dr(f"b1{n}"), 1)
            for s in range(2):
                wait_drained(v, f"od{s}")
            norm_stats([2])
            v.wait_ge(o_std, 2)
            me.done(V.reciprocal(rs[0:DEC, 1, 2 * H:3 * H], rs[0:DEC, 0, 2 * H:3 * H]))
            me.settle()
            normalise(2)
            for n in range(NB):
                wait_drained(v, f"g{n}")
            for n in range(NB):
                wait_filled(v, f"ot{n}")
                tt(oT[:, n, :], bank(f"ot{n}")[:, 0:T], gT[:, n, :], ALU.mult).then_inc(dr(f"ot{n}"), 1)
            for n in range(NB):
                wait_drained(v, f"m{n}")
                wait_drained(v, f"b1{n}")
            for n in range(NB):
                wait_filled(v, f"b0{n}")
                me.done(tt(mgla[:, n, :], bank(f"b0{n}")[:, 0:T], mgla[:, n, :], ALU.mult))
                me.settle()
                tt(merged[:, n, :], merged[:, n, :], mgla[:, n, :], ALU.add).then_inc(dr(f"b0{n}"), 1)
            v.wait_ge(x_landed, 16)
            for n in range(NB):
                wait_filled(v, f"wo{n}")
                stt(yT[:, n, :], x_in[:, n, :], ALPHA, bank(f"wo{n}")[:, 0:T], ALU.mult, ALU.add).then_inc(dr(f"wo{n}"), 1)

            def layer_norm(src, var_sem, std_sem, norm_sem, gain, done_sem, dst, landed):
                for t, (first, rows) in enumerate(TILES):
                    landed(t)
                    for s in range(2):
                        me.done(V.bn_stats(st1[0:rows, t, s, :], src[0:rows, t, s * 512:(s + 1) * 512]))
                    me.settle()
                    me.done(V.bn_aggr(mv1[0:rows, t, :], st1[0:rows, t, :, :].rearrange("p a b -> p (a b)")))
                    me.settle()
                    ts(rs1[0:rows, 0, t:t + 1], mv1[0:rows, t, 1:2], EPS, None, ALU.add).then_inc(var_sem, 1)
                for t, (first, rows) in enumerate(TILES):
                    v.wait_ge(std_sem, t + 1)
                    me.done(V.reciprocal(rs1[0:rows, 1, t:t + 1], rs1[0:rows, 0, t:t + 1]))
                    me.settle()
                    ts(src[0:rows, t, :], src[0:rows, t, :], mv1[0:rows, t, 0:1], rs1[0:rows, 1, t:t + 1],
                       ALU.subtract, ALU.mult).then_inc(norm_sem, 1)
                    if src is not dst:
                        continue
                    v.wait_ge(norm_sem, t + 1)
                    me.done(tt(dst[0:rows, t, :], src[0:rows, t, :], gain[0:rows, 0, :], ALU.mult))
                    me.settle()
                    tt(dst[0:rows, t, :], dst[0:rows, t, :], gain[0:rows, 1, :], ALU.add).then_inc(done_sem, 1)

            def y_landed(t):
                for s in range(2):
                    wait_drained(v, f"yt{t}{s}")

            layer_norm(ytok, y_var, y_std, y_norm, None, None, x1, y_landed)
            v.wait_ge(y_norm, NT)
            v.wait_ge(ln_in, 32)
            for t, (first, rows) in enumerate(TILES):
                me.done(tt(x1[0:rows, t, :], ytok[0:rows, t, :], ln1[0:rows, 0, :], ALU.mult))
                me.settle()
                tt(x1[0:rows, t, :], x1[0:rows, t, :], ln1[0:rows, 1, :], ALU.add).then_inc(x1_done, 1)
            for t in (sel, ex, wtx):
                me.done(V.memset(t[:, :, :], 0.0))
            v.wait_ge(rb_in, 16)
            me.settle()
            wait_filled(v, "lg")
            me.done(tt(lg[:, 0:2, :], bank("lg")[:, 0:2 * E].rearrange("p (t e) -> p t e", e=E),
                       rb[:, :].unsqueeze(1).to_broadcast([P, 2, E]), ALU.add))
            tt(lg[0:DEC, 2, :], bank("lg")[0:DEC, 2 * E:3 * E], rb[0:DEC, :], ALU.add).then_inc(dr("lg"), 1)
            wait_drained(v, "lg")
            me.settle()
            for t, (first, rows) in enumerate(TILES):
                me.done(V.max(mx[0:rows, t, :], lg[0:rows, t, :]))
                me.settle()
                ts(red[0:rows, 0, t:t + 1], mx[0:rows, t, 0:1], -1.0, None, ALU.mult).then_inc(lg_done, 1)
                fourth = mx[0:rows, t, 3:4]
                me.done(ts(eq[0:rows, t, :], lg[0:rows, t, :], fourth, None, ALU.is_equal))
                me.done(ts(sel[0:rows, t, :], lg[0:rows, t, :], fourth, None, ALU.is_gt))
                me.settle()
                me.done(V.tensor_tensor_scan(cum[0:rows, t, :], ones[0:rows, 0:E], eq[0:rows, t, :], 0.0, ALU.mult, ALU.add))
                me.done(V.reduce_sum(red[0:rows, 1, t:t + 1], sel[0:rows, t, :], AX_X))
                me.settle()
                me.done(ts(red[0:rows, 2, t:t + 1], red[0:rows, 1, t:t + 1], -1.0, 4.0, ALU.mult, ALU.add))
                me.settle()
                me.done(stt(eq[0:rows, t, :], cum[0:rows, t, :], red[0:rows, 2, t:t + 1], eq[0:rows, t, :],
                            ALU.is_le, ALU.mult))
                me.settle()
                me.done(tt(sel[0:rows, t, :], sel[0:rows, t, :], eq[0:rows, t, :], ALU.add))
            me.settle()
            V.memset(pick[0:1, 0, 0:1], 0.0).then_inc(sel_done, 1)
            for t, (first, rows) in enumerate(TILES):
                v.wait_ge(ex_done, t + 1)
                me.done(tt(ex[0:rows, t, :], ex[0:rows, t, :], sel[0:rows, t, :], ALU.mult))
                me.settle()
                me.done(V.reduce_sum(red[0:rows, 1, t:t + 1], ex[0:rows, t, :], AX_X))
                me.settle()
                me.done(V.reciprocal(red[0:rows, 3, t:t + 1], red[0:rows, 1, t:t + 1]))
                me.settle()
                me.done(ts(wtx[0:rows, t, 0:E], ex[0:rows, t, :], red[0:rows, 3, t:t + 1], None, ALU.mult))
            me.settle()
            V.memset(pick[0:1, 0, 0:1], 0.0).then_inc(wt_done, 1)
            wait_filled(v, "rk")
            me.done(ts(eq[:, :, :], sel[:, :, :], -FAR, FAR, ALU.mult, ALU.add))
            me.settle()
            me.done(tt(rankx[:, :, 0:E], eq[:, :, :], bank("rk")[:, 0:NT * E].rearrange("p (t e) -> p t e", e=E), ALU.add))
            V.reduce_max(red[:, 0, 0:1], bank("rk")[:, NT * E:(NT + 1) * E], AX_X).then_inc(dr("rk"), 1)
            wait_drained(v, "rk")
            ts(flag[:, :], red[:, 0, 0:1], float(CAP), None, ALU.is_gt).then_inc(flag_done, 1)
            for p in range(1, PASSES + 1):
                me.done(ts(rankx[:, :, p * E:(p + 1) * E], rankx[:, :, 0:E], -float(CAP * p), None, ALU.add))
                me.done(V.tensor_copy(wtx[:, :, p * E:(p + 1) * E], wtx[:, :, 0:E]))
            me.settle()
            iota4 = iota[:, :].unsqueeze(1).unsqueeze(1).to_broadcast([P, NT, 2, CAP])

            def choose(first):
                tt(pick.rearrange("p t (j c) -> p t j c", j=2), iota4,
                   rankx[:, :, first].unsqueeze(3).to_broadcast([P, NT, 2, CAP]), ALU.is_equal).then_inc(picked, 1)

            choose(slice(0, 2))
            wait_filled(v, "wt")
            V.tensor_copy(wT[:, :], bank("wt")[0:E, 0:T]).then_inc(dr("wt"), 1)
            for n in range(NB):
                wait_filled(v, f"bd{n}")
                V.tensor_copy(yacc[:, n, :], bank(f"bd{n}")[:, 0:T]).then_inc(dr(f"bd{n}"), 1)
            for n in range(NB):
                wait_drained(v, f"bd{n}")
            V.memset(gbuf[0:1, 1:2], 0.0).then_inc(gu_read, 1)
            V.memset(gbuf[0:1, 2:3], 0.0).then_inc(scat_read, 1)
            v.wait_ge(pool_c, 15)

            def one_hot(first):
                ts(oh[:, :], which[:, :], eid[:, first], None, ALU.is_equal).then_inc(oh_ready, 1)

            v.wait_ge(b3_step, 9)
            one_hot(slice(0, 1))
            steps = {}

            def body(it, pair, tag):
                me.n, start = 0, steps["base"]
                me.base = (it - steps["first"]) * STEP + start
                v.wait_ge(picked, it + 1)
                for x in range(2):
                    last = tt(wpick[:, :, x, :, :], pick[:, :, x * CAP:(x + 1) * CAP].unsqueeze(2).to_broadcast([P, NT, 2, CAP]),
                              wtx[:, :, bass.ds(pair * 2 + x, 1)].unsqueeze(3).to_broadcast([P, NT, 2, CAP]), ALU.mult)
                last.then_inc(wpicked, 1)
                v.wait_ge(wpicked, it + 1)
                v.wait_ge(gath_done, it * 2 + 2)
                choose(bass.ds(it * 2 + 2, 2))
                for j in range(2):
                    n = it * 2 + j
                    e = pair * 2 + j
                    v.wait_ge(gu_used, n * NB + 2 * NB)
                    ts(gbuf, GATE, LIMIT, None, ALU.min).then_inc(gclip, 1)
                    ts(ubuf, UP, LIMIT, -LIMIT, ALU.min, ALU.max).then_inc(gu_read, 1)
                    one_hot(bass.ds(e + 1, 1))
                    v.wait_ge(gclip, n + 1)
                    v.wait_ge(gu_read, n + 2)
                    me.done(stt(tbuf, ubuf, 1.0, gbuf, ALU.add, ALU.mult))
                    me.settle()
                    v.wait_ge(sig_done, n + 1)
                    tt(act_s, tbuf, sbuf_, ALU.mult).then_inc(act_ready, 1)
                    if j == 0:
                        v.wait_ge(scat_done, it * 5 + 1)
                        V.tensor_copy(swT, SCAT[:, :, 0:T]).then_inc(scat_read, 1)
                for d in range(4):
                    v.wait_ge(scat_done, it * 5 + 2 + d)
                    tt(yacc[:, d:NB:4, :], yacc[:, d:NB:4, :], (SCAT if d % 2 == 0 else SCAT2)[:, :, 0:T], ALU.add
                       ).then_inc(scat_read, 1)
                assert me.n == STEP, me.n

            STEP = 2
            steps["base"], steps["first"] = me.n, 0
            with v.Fori(0, PAIRS) as pair:
                body(pair, pair, 0)
            v.wait_ge(flag_done, 1)
            over = v.value_load(flag[0:1, 0:1], min_val=0, max_val=1)
            with v.If(over == 1):
                with v.Fori(1, PASSES) as turn_:
                    with v.Fori(0, PAIRS) as pair:
                        body(turn_ * PAIRS + pair, pair, 1)
            V.memset(mx[0:1, 0, 0:1], 0.0).then_inc(moe_done, 1)
            me.s, me.n, me.base = tail, 0, 0
            v.wait_ge(ln2_in, 32)
            u = 0
            for t, (first, rows) in enumerate(TILES):
                for s in range(2):
                    v.wait_ge(fin_full, u + 1)
                    cols = slice(s * 512, (s + 1) * 512)
                    stt(y2[0:rows, t, cols], x1[0:rows, t, cols], ALPHA, pool4[0:rows, u % 2, :], ALU.mult, ALU.add
                        ).then_inc(fin_read, 1)
                    u += 1

            def y2_landed(t):
                v.wait_ge(fin_read, 2 * t + 2)

            layer_norm(y2, y2_var, y2_std, y2_norm, ln2, y2_done, y2, y2_landed)


_NAMES = ("xT", "w_in", "w_branch", "w_o", "gla_w_a2", "rg_w_a", "rg_w_x", "state_gla", "pack", "moe_b_gu", "ln1_g", "ln1_b",
          "ln2_g", "ln2_b", "router_b", "moe_w_gu", "moe_w_down", "moe_b_down")
_OUTS = (("y_prompt", (1, SEQ, D)), ("y_sample", (DEC, 1, D)), ("gla_prompt", (1, 1, H, DK, DV)),
         ("gla_sample", (1, DEC, H, DK, DV)), ("small", (P, NOUT)))


def kernel(**inputs):
    import numpy as np
    import concourse.bacc as bacc
    from concourse.bass_utils import run_bass_kernel_spmd as run

    x = {k: np.asarray(v) for k, v in inputs.items()}

    def channels(a):
        a = np.moveaxis(a, -1, 0)
        a = a.reshape((-1, P) + a.shape[1:])
        return np.moveaxis(a, 1, 0)

    tokens = np.concatenate([x["x_prompt"][0], x["x_sample"][:, 0]], axis=0)
    parts = {
        "conv_w": channels(x["rg_conv_w"][0]), "conv_b": channels(x["rg_conv_b"][0]),
        "b_r": channels(x["rg_b_a"][0]), "b_i": channels(x["rg_b_x"][0]), "lam": channels(x["rg_lambda"][0]),
        "b_a": channels(x["gla_b_a"][0]), "norm_g": channels(x["gla_norm_g"][0]),
        "b_merge": channels(x["b_merge"][0]), "h0": channels(x["state_rglru"][0]),
        "conv0": channels(x["state_conv"][0]),
        "router_w": channels(np.swapaxes(x["router_w"][0], 0, 1)),
        "ln1_g": channels(x["ln1_g"][0]), "ln1_b": channels(x["ln1_b"][0]),
    }
    x["pack"] = np.concatenate([parts[n].reshape(P, -1) for n in PACK], axis=1)
    x["xT"] = channels(tokens)

    nc = bacc.Bacc("TRN2", target_bir_lowering=False, num_devices=1)
    arrays, args = {}, []
    for name in _NAMES:
        a = np.ascontiguousarray(x[name])
        arrays[f"in_{name}"] = a
        args.append(nc.dram_tensor(f"in_{name}", a.shape, mybir.dt.from_np(a.dtype), kind="ExternalInput").ap())
    for name, shape in _OUTS:
        args.append(nc.dram_tensor(f"out_{name}", shape, F32, kind="ExternalOutput").ap())
    build(nc, *args)
    got = run(nc, [arrays], core_ids=[0]).results[0]
    small = got["out_small"]

    def rows(a, inner):
        a = a.reshape((P, NB) + inner)
        return np.moveaxis(a, (1, 0), (-2, -1)).reshape(inner + (D,))

    conv_p = rows(small[:, OUT_CONVP:OUT_CONVS], (CW - 1,))[None, None]
    conv_s = rows(small[:, OUT_CONVS:OUT_HP], (DEC, CW - 1))[None]
    h_p = rows(small[:, OUT_HP:OUT_HS], (1,))[None]
    h_s = rows(small[:, OUT_HS:NOUT], (DEC,))[None]
    return (got["out_y_prompt"], got["out_y_sample"], got["out_gla_prompt"], h_p, conv_p, got["out_gla_sample"],
            h_s, conv_s)
```

```python
from contextlib import ExitStack

import concourse.bass as bass
from concourse import mybir

F32 = mybir.dt.float32
BF16 = mybir.dt.bfloat16
F32R = mybir.dt.float32r
I32 = mybir.dt.int32
ALU = mybir.AluOpType
ACT = mybir.ActivationFunctionType
AX_X = mybir.AxisListType.X

P = 128
D = 1024
NB = D // P
SEQ, DEC = 256, 8
T = SEQ + DEC
H, DK, DV = 4, 128, 256
CH = 64
NCH = SEQ // CH
RANK = 16
CW = 4
CIN = CW - 1 + SEQ + DEC * CW
COUT = CIN - (CW - 1)
E = 32
SPLITS = 3
CAP = 64
PAIRS = E // 2
PASSES = -(-T // CAP)
F = D
ALPHA = 2.0 ** 0.25
EPS = 1e-5
LIMIT, SWISH = 7.0, 1.702
TILES = [(0, P), (P, P), (2 * P, DEC)]
NT = len(TILES)
FAR = 4096.0
WCOL = 256
SLOT = NB * T

PACK = {}
_at = 0
for _n, _w in (("conv_w", NB * CW), ("conv_b", NB), ("b_r", NB), ("b_i", NB), ("lam", NB), ("b_a", H),
               ("norm_g", NB), ("b_merge", 2 * NB), ("h0", NB * DEC), ("conv0", NB * DEC * (CW - 1)),
               ("router_w", NB * E), ("ln1_g", NB), ("ln1_b", NB)):
    PACK[_n] = (_at, _w)
    _at += _w
NPACK = _at
OUT_CONVP, OUT_CONVS, OUT_HP, OUT_HS = 0, 24, 24 + 192, 24 + 192 + 8
NOUT = OUT_HS + NB * DEC


def mixer_jobs():
    jobs = [f"xr{n}" for n in range(NB)] + ["low"]
    jobs += [f"k{n}" for n in range(H)]
    for n in range(NB):
        jobs += [f"r{n}", f"i{n}"]
    jobs += [f"q{n}" for n in range(H)] + [f"v{n}" for n in range(NB)]
    jobs += [f"z{n}" for n in range(H)] + [f"g{n}" for n in range(NB)]
    jobs += [f"vt{t}{s}" for t in range(NT) for s in range(2)] + [f"kt{t}" for t in range(NT)] + ["sc"]
    jobs += [f"m{n}" for n in range(2 * NB)] + [f"b1{n}" for n in range(NB)]
    jobs += [f"ot{n}" for n in range(NB)] + [f"b0{n}" for n in range(NB)]
    jobs += [f"wo{n}" for n in range(6)] + [f"yt{t}0" for t in range(NT)]
    jobs += [f"wo{n}" for n in range(6, NB)] + [f"yt{t}1" for t in range(NT)]
    jobs += [f"xt{n}" for n in range(4)] + [f"xt{n}" for n in range(4, NB)] + ["lg", "rk"]
    return jobs


def build(nc, xT, w_in, w_branch, w_o, gla_w_a2, rg_w_a, rg_w_x, state_gla, pack, b_gu, ln1_g, ln1_b, ln2_g, ln2_b,
          router_b, w_gu, w_down, b_down, y_prompt, y_sample, gla_prompt, gla_sample, small):
    jobs = mixer_jobs()
    job = {n: i for i, n in enumerate(jobs)}

    q0, k0, v0, g0 = 0, H * DK, 2 * H * DK, 2 * H * DK + D
    low0 = g0 + D
    xr0 = low0 + RANK
    m0 = xr0 + D
    tiles = []

    def add_tiles(name, matrix, col, blocks):
        for b in range(0, blocks, 2):
            tiles.append((name, b, matrix, col + b * P))

    add_tiles("xr", w_in[0], xr0, NB)
    add_tiles("k", w_in[0], k0, H)
    add_tiles("q", w_in[0], q0, H)
    add_tiles("v", w_in[0], v0, NB)
    add_tiles("g", w_in[0], g0, NB)
    add_tiles("m", w_in[0], m0, 2 * NB)
    add_tiles("b1", w_branch[0, 1], 0, NB)
    add_tiles("b0", w_branch[0, 0], 0, NB)
    add_tiles("wo", w_o[0], 0, NB)
    tile_of = {f"{n}{b + j}": (i, j) for i, (n, b, _, _) in enumerate(tiles) for j in range(2)}

    split_jobs = [f"{n}{b}" for n, m in (("xr", NB), ("k", H), ("q", H), ("v", NB), ("g", NB), ("m", 2 * NB),
                                         ("b1", NB), ("b0", NB), ("wo", NB)) for b in range(m)]
    NSPLIT = len(split_jobs)
    NX = NSPLIT - 3 * NB
    split_of = {n: p for p, n in enumerate(split_jobs)}

    with ExitStack() as ctx:
        def sb(name, shape, dt=F32):
            return ctx.enter_context(nc.sbuf_tensor(name, shape, dt))

        def ps(name, shape):
            return ctx.enter_context(nc.psum_tensor(name, shape, F32))

        def sem(name):
            return ctx.enter_context(nc.semaphore(name))

        gu_at = -(-nc.sbuf_base // 32) * 32
        gu_w = sb("gu_w", [P, NB, 2 * F])
        dn_w = sb("dn_w", [P, NB, D])
        ring = dn_w[:, :, :].rearrange("p (s a) n -> p s (a n)", a=2).rearrange("p s (k n) -> p s k n", n=WCOL)
        gate_w = gu_w[:, 7, :].rearrange("p (w n d) -> p w n d", w=2, n=NB)
        dstate = [gu_w[:, 5 + i // 2, (i % 2) * D:(i % 2 + 1) * D] for i in range(4)]
        x_in = sb("x_in", [P, NB, T])
        WB = NB * P
        xh = nc.alloc_sbuf_tensor_at("xh", [P, NB, T], F32R, offset=gu_at + 4 * (NB * 2 * F + NB * D))
        wh = [nc.alloc_sbuf_tensor_at(f"wh{i}", [P, NB, P], F32R, offset=gu_at + 8 * i * WB) for i in range(SPLITS)]
        wl = [nc.alloc_sbuf_tensor_at(f"wl{i}", [P, NB, P], F32R, offset=gu_at + 8 * i * WB + 4 * WB) for i in range(SPLITS)]
        xl_most = nc.alloc_sbuf_tensor_at("xl_most", [P, NB - 1, T], F32R, offset=gu_at + 8 * SPLITS * WB)
        xl_rest = sb("xl_rest", [P, T], F32R)
        xl = [xl_most[:, k, :] for k in range(NB - 1)] + [xl_rest[:, :]]
        arena = sb("arena", [P, 10 * SLOT])

        def slot(i, first=0, size=SLOT):
            return arena[:, i * SLOT + first:i * SLOT + first + size]

        def blocks(ap, n):
            return ap.rearrange("p (n t) -> p n t", n=n)

        HALF = H * T
        cin = blocks(slot(0, 0, NB * CIN), NB)
        xc = blocks(slot(2), NB)
        rgate = blocks(slot(3), NB)
        x_raw = blocks(slot(4), NB)
        igate = blocks(slot(4), NB)
        decay = blocks(slot(5), NB)
        root = blocks(slot(6), NB)
        ctmp = slot(6, 0, 2 * COUT).rearrange("p (a n) -> p a n", a=2)
        hs = blocks(slot(7), NB)
        kT = blocks(slot(8, 0, HALF), H)
        qT = blocks(slot(8, HALF, HALF), H)
        vT = blocks(slot(9), NB)
        za = blocks(slot(2, 0, HALF), H)
        zb = blocks(slot(2, HALF, HALF), H)
        bc = blocks(slot(3, 0, HALF), H)
        eb = blocks(slot(3, HALF, HALF), H)
        enb = blocks(slot(5, 0, HALF), H)
        kd = blocks(slot(5, HALF, HALF), H)
        qe = blocks(slot(4, 0, HALF), H)
        ke = blocks(slot(4, HALF, HALF), H)
        gT = blocks(slot(6), NB)
        vtok = slot(0, 0, NT * D).rearrange("p (t n) -> p t n", t=NT)
        kdt = slot(2, 0, NT * H * DK).rearrange("p (t n) -> p t n", t=NT)
        scs = slot(2, NT * H * DK, 8 * CH).rearrange("p (g t) -> p g t", t=CH)
        otok = slot(8, 0, NT * D).rearrange("p (t n) -> p t n", t=NT)
        mgla = blocks(slot(3), NB)
        mrg = blocks(slot(5), NB)
        oT = blocks(slot(4), NB)
        merged = blocks(slot(2), NB)
        x_res = blocks(slot(6), NB)
        yT = blocks(slot(0), NB)
        ytok = slot(8, 0, NT * D).rearrange("p (t n) -> p t n", t=NT)
        x1 = slot(5, 0, NT * D).rearrange("p (t n) -> p t n", t=NT)
        x1T = blocks(slot(4), NB)
        ln1 = slot(7, 0, 2 * D).rearrange("p (a n) -> p a n", a=2)
        ln2 = slot(3, 0, 2 * D).rearrange("p (a n) -> p a n", a=2)
        yacc = blocks(slot(4), NB)
        xg = blocks(slot(2, 0, NB * 2 * CAP), NB)
        HF = F // 2
        x_flat = x_in[:, :, :].rearrange("p n t -> p (n t)")
        eo = x_flat[:, 0:D]
        wpick = x_flat[:, D:D + NT * 2 * CAP].rearrange("p (t c) -> p t c", t=NT)
        pick = x_flat[:, D + 384:D + 384 + NT * CAP].bitcast(BF16).rearrange("p (t c) -> p t c", t=NT)
        swT = x_flat[:, D + 576:D + 576 + T]
        gbuf, ubuf, tbuf, sbuf_ = (slot(8, i * HF, HF) for i in range(4))
        act_s = slot(9, 0, HF)
        act_t = slot(2, D, HF).rearrange("p (c s) -> p c s", c=4)
        xparts = [[slot(0, (3 * t + part) * HF, HF).bitcast(BF16) for part in range(3)] for t in range(2)]
        xparts.append([slot(9, 960, HF).bitcast(BF16), slot(9, 960 + HF, HF).bitcast(BF16),
                       slot(2, D + HF, HF).bitcast(BF16)])
        b3 = slot(1, 1024, F).bitcast(BF16)[0:3 * E, :]
        braw = gu_w[0:3 * E, 4, :]
        y2 = slot(0, 0, NT * D).rearrange("p (t n) -> p t n", t=NT)

        consts = sb("consts", [P, NPACK])

        def con(name):
            a, w = PACK[name]
            return consts[:, a:a + w]

        conv_w, conv_b = blocks(con("conv_w"), NB), con("conv_b")
        router_w = blocks(con("router_w"), NB)
        ident = sb("ident", [P, P])
        before = sb("before", [P, P])
        ones = sb("ones", [P, P])
        causal = sb("causal", [P, CH])
        keep = sb("keep", [P, T])
        iota = sb("iota", [P, CAP])
        low_w = sb("low_w", [P, NB, RANK])
        a2 = sb("a2", [RANK, H * DK])
        lowT = sb("lowT", [RANK, T])
        rb = sb("rb", [P, E])
        Sg = sb("Sg", [P, H, DV])
        km = slot(9, 1088, 2 * H * DK)[0:DEC, :].rearrange("p (a n) -> p a n", a=2)
        rest = [ytok[:, 0, :], ytok[:, 1, :], Sg[:, :, :].rearrange("p h v -> p (h v)")]
        ebl = sb("ebl", [P, H, NCH])
        ebd = sb("ebd", [P, H, DEC])
        qd = keep[:, 0:H * DEC * DEC].rearrange("p (h b c) -> p h b c", h=H, b=DEC)
        sp_ = sb("sp_", [P, 5, NB])
        st = sb("st", [P, NT, H, 6])
        mv = sb("mv", [P, NT, H, 2])
        rs = sb("rs", [P, 2, NT * H])
        st1 = sb("st1", [P, NT, 2, 6])
        mv1 = sb("mv1", [P, NT, 2])
        rs1 = sb("rs1", [P, 2, NT])
        outs = sb("outs", [P, NOUT])
        lg = sb("lg", [P, NT, E])
        mx = sb("mx", [P, NT, 8])
        eq = sb("eq", [P, NT, E])
        cum = sb("cum", [P, NT, E])
        cum2 = sb("cum2", [P, NT, E])
        sel = sb("sel", [P, NT, E])
        ex = sb("ex", [P, NT, E])
        red = sb("red", [P, 4, NT])
        flag = sb("flag", [P, 1], I32)
        lgT = slot(6, 1100, T)[0:E, :]
        before16 = sb("before16", [P, P], BF16)
        ones16 = sb("ones16", [P, P], BF16)
        sel16 = sb("sel16", [P, NT, E], BF16)
        NRX = (PASSES + 1) * E
        routes = slot(5, NT * D, 2 * NT * NRX)
        rankx = routes[:, 0:NT * NRX].rearrange("p (t e) -> p t e", t=NT)
        wtx = routes[:, NT * NRX:2 * NT * NRX].rearrange("p (t e) -> p t e", t=NT)
        keep3 = sb("keep3", [P, NT * E])
        which = sb("which", [3 * E, CAP])
        eid = sb("eid", [3 * E, E + 1])
        oh = sb("oh", [3 * E, CAP], BF16)

        pool4 = ps("pool4", [P, 4, 512])
        ub = ps("ub", [P, 2, 512])
        ob = ps("ob", [P, 2, 512])
        GATE, UP, DOWN, ACTT = (pool4[:, i, :] for i in range(4))
        GATH, SCAT, SCAT2 = ub, ob, ub

        last_bank = [ub[:, 0, :], ub[:, 1, :], ob[:, 1, :], pool4[:, 2, :], pool4[:, 3, :], ob[:, 0, :]]

        tile_in = [sem(f"tile_in{i}") for i in range(4)]
        filled = [sem(f"filled{i}") for i in range(4)]
        drained = [sem(f"drained{i}") for i in range(4)]
        x_hi, x_lo, w_hi, w_lo_first, w_lo = (sem(n) for n in ("x_hi", "x_lo", "w_hi", "w_lo_first", "w_lo"))
        b_rest = sem("b_rest")
        x_again = sem("x_again")
        x_landed, pack_in, low_in, a2_in, gate_in = (sem(n) for n in ("x_landed", "pack_in", "low_in", "a2_in", "gate_in"))
        ln_in, ln2_in, rb_in, bdn_in = (sem(n) for n in ("ln_in", "ln2_in", "rb_in", "bdn_in"))
        dst_in = [sem(f"dst_in{i}") for i in range(4)]
        dst_out = [sem(f"dst_out{i}") for i in range(4)]
        stored = sem("stored")
        stored_early = sem("stored_early")
        pool_c = sem("pool_c")
        dve = sem("dve_step")
        act = sem("act_step")
        conv_done, rg_exp, rg_root, rg_rooted, rg_done = (sem(n) for n in ("conv_done", "rg_exp", "rg_root", "rg_rooted", "rg_done"))
        z_abs, z_min, z_ln, b_done, b_exp, gla_in = (sem(n) for n in ("z_abs", "z_min", "z_ln", "b_done", "b_exp", "gla_in"))
        gsig = sem("gsig")
        o_full, o_read, u_full, s_done = (sem(n) for n in ("o_full", "o_read", "u_full", "s_done"))
        km_done, d_full, d_done, od_full, od_sb = (sem(n) for n in ("km_done", "d_full", "d_done", "od_full", "od_sb"))
        o_var, o_std, o_norm = (sem(n) for n in ("o_var", "o_std", "o_norm"))
        y_var, y_std, y_norm, x1_done = (sem(n) for n in ("y_var", "y_std", "y_norm", "x1_done"))
        lg_done, ex_done, sel_done, flag_done = (sem(n) for n in ("lg_done", "ex_done", "sel_done", "flag_done"))
        small_done = sem("small_done")
        gu_in = [sem(f"gu_in{k}") for k in range(NB)]
        dn_in = [sem(f"dn_in{k}") for k in range(NB)]
        gu_used, dn_used = sem("gu_used"), sem("dn_used")
        braw_in, b3_step, oh_ready = sem("braw_in"), sem("b3_step"), sem("oh_ready")
        eo_last, xp_hi, xp_mid, xp_lo, xp_r1, xp_r2 = (
            sem(n) for n in ("eo_last", "xp_hi", "xp_mid", "xp_lo", "xp_r1", "xp_r2"))
        eo_zero, x1_small, xp_zero, xp_r1_small = (sem(n) for n in ("eo_zero", "x1_small", "xp_zero", "xp_r1_small"))
        lgt_full, lgt_read = sem("lgt_full"), sem("lgt_read")
        swt_last, last_full, scat_last = (sem(n) for n in ("swt_last", "last_full", "scat_last"))
        act_tr, actt_ready = sem("act_tr"), sem("actt_ready")
        picked, wpicked = sem("picked"), sem("wpicked")
        gath_done, xg_ready = sem("gath_done"), sem("xg_ready")
        gu_read, gclip, sig_done, act_ready = (sem(n) for n in ("gu_read", "gclip", "sig_done", "act_ready"))
        eo_ready, scat_done, scat_read = (sem(n) for n in ("eo_ready", "scat_done", "scat_read"))
        moe_done, fin_full, fin_read, y2_var, y2_std, y2_done, tail = (
            sem(n) for n in ("moe_done", "fin_full", "fin_read", "y2_var", "y2_std", "y2_done", "tail_step"))

        def bank(name):
            return pool4[:, job[name] % 4, :]

        def open_job(eng, name):
            i = job[name]
            if i >= 4:
                eng.wait_ge(drained[i % 4], i // 4)

        def wait_filled(eng, name):
            eng.wait_ge(filled[job[name] % 4], job[name] // 4 + 1)

        def wait_drained(eng, name):
            eng.wait_ge(drained[job[name] % 4], job[name] // 4 + 1)

        fl = lambda name: filled[job[name] % 4]
        dr = lambda name: drained[job[name] % 4]

        def raw_block(p):
            i, half = tile_of[split_jobs[p]]
            return ring[:, i % 4, :, half * P:(half + 1) * P]

        def wait_raw(eng, p):
            i = tile_of[split_jobs[p]][0]
            eng.wait_ge(tile_in[i % 4], 16 * (i // 4 + 1))

        class Steps:
            def __init__(self, eng, s):
                self.eng, self.s, self.n, self.base = eng, s, 0, 0

            def done(self, ins):
                ins.then_inc(self.s, 1)
                self.n += 1

            def settle(self):
                self.eng.wait_ge(self.s, self.base + self.n)

        def moe_loops(eng, body):
            with eng.Fori(0, PAIRS) as pair:
                body(pair, pair)
            eng.wait_ge(flag_done, 1)
            over = eng.value_load(flag[0:1, 0:1], min_val=0, max_val=1)
            with eng.If(over == 1):
                with eng.Fori(1, PASSES) as turn:
                    with eng.Fori(0, PAIRS) as pair:
                        body(turn * PAIRS + pair, pair)

        block = ctx.enter_context(nc.Block())

        @block.sync
        def _(sp):
            sp.dma_start(x_raw, xT).then_inc(x_landed, 16)
            for i, (name, b, matrix, col) in enumerate(tiles):
                if i >= 4:
                    former = tiles[i - 4]
                    wait_filled(sp, f"{former[0]}{former[1] + 1}")
                sp.dma_start(ring[:, i % 4, :, :],
                             matrix[:, col:col + WCOL].rearrange("(k p) n -> p k n", p=P)).then_inc(tile_in[i % 4], 16)
                if i == 0:
                    sp.dma_start(consts[:, :], pack).then_inc(pack_in, 16)
                    sp.dma_start(low_w[:, :, :], w_in[0, :, low0:low0 + RANK].rearrange("(k p) n -> p k n", p=P)
                                 ).then_inc(low_in, 16)
                    sp.dma_start(a2[:, :], gla_w_a2[0]).then_inc(a2_in, 16)
                if name == "wo" and b == 0:
                    wait_drained(sp, f"ot{NB - 1}")
                    sp.dma_start(x_res, xT).then_inc(x_again, 16)
                if i == 2:
                    for part in range(3):
                        sp.dma_start(braw[part * E:(part + 1) * E, :], b_gu[0]).then_inc(braw_in, 16)
                if i == 1:
                    sp.dma_start(gate_w[:, 0, :, :], rg_w_a[0].rearrange("n c d -> c n d")).then_inc(gate_in, 16)
                    sp.dma_start(gate_w[:, 1, :, :], rg_w_x[0].rearrange("n c d -> c n d")).then_inc(gate_in, 16)
            sp.wait_ge(b3_step, 3)
            for i in range(4):
                sp.wait_ge(dst_out[i], 32)

            def body(it, pair):
                for j in range(2):
                    n = it * 2 + j
                    for k in range(NB):
                        sp.wait_ge(gu_used, n * NB + k + 1)
                        sp.dma_start(gu_w[:, k, :], w_gu[0, bass.ds(pair * 2 + j, 1), k * P:(k + 1) * P, :]
                                     .rearrange("e p n -> (e p) n")).then_inc(gu_in[k], 16)
                    for k in range(NB):
                        sp.wait_ge(dn_used, n * NB + k + 1)
                        sp.dma_start(dn_w[:, k, :], w_down[0, bass.ds(pair * 2 + j, 1), k * P:(k + 1) * P, :]
                                     .rearrange("e p n -> (e p) n")).then_inc(dn_in[k], 16)

            moe_loops(sp, body)
            for t, (first, rows) in enumerate(TILES):
                sp.wait_ge(y2_done, t + 1)
                dst = y_prompt[0, first:first + rows, :] if t < 2 else y_sample.rearrange("b s d -> (b s) d")
                sp.dma_start(dst, y2[0:rows, t, :]).then_inc(stored, 16)
            sp.wait_ge(stored, 16 * NT)

        @block.gpsimd
        def _(pool):
            g = nc.gpsimd
            g.memset(ident[:, :], 0.0).then_inc(pool_c, 1)
            g.memset(ones[:, :], 1.0).then_inc(pool_c, 1)
            g.memset(keep[:, :], 1.0).then_inc(pool_c, 1)
            g.iota(iota[:, :], pattern=[[1, CAP]], base=0, channel_multiplier=0,
                   allow_small_or_imprecise_dtypes=True).then_inc(pool_c, 1)
            pool.wait_ge(pool_c, 4)
            g.affine_select(out=ident[:, :], in_=ident[:, :], compare_op=ALU.not_equal, fill=1.0, base=0,
                            pattern=[[-1, P]], channel_multiplier=1).then_inc(pool_c, 1)
            g.affine_select(out=before[:, :], in_=ones[:, :], compare_op=ALU.is_gt, fill=0.0, base=0,
                            pattern=[[1, P]], channel_multiplier=-1).then_inc(pool_c, 1)
            for c in range(2):
                pool.wait_ge(pool_c, 6 + c)
                g.affine_select(out=causal[c * CH:(c + 1) * CH, :], in_=ones[c * CH:(c + 1) * CH, 0:CH],
                                compare_op=ALU.is_ge, fill=0.0, base=0, pattern=[[1, CH]],
                                channel_multiplier=-1).then_inc(pool_c, 1)
            pool.wait_ge(pool_c, 8)
            g.memset(keep[:, 0:SEQ:CH], 0.0).then_inc(pool_c, 1)
            g.memset(keep[:, SEQ:T], 0.0).then_inc(pool_c, 1)
            for part in range(3):
                pool.wait_ge(pool_c, 10 + part)
                g.iota(which[part * E:(part + 1) * E, :], pattern=[[0, CAP]], base=0, channel_multiplier=1,
                       allow_small_or_imprecise_dtypes=True).then_inc(pool_c, 1)
            pool.wait_ge(pool_c, 13)
            g.iota(eid[:, 0:E], pattern=[[1, E]], base=0, channel_multiplier=0,
                   allow_small_or_imprecise_dtypes=True).then_inc(pool_c, 1)
            pool.wait_ge(pool_c, 14)
            g.memset(eid[:, E:E + 1], 0.0).then_inc(pool_c, 1)

            def low_part(p):
                pool.wait_ge(w_hi, p + 1)
                if p > 2:
                    pool.wait_ge(w_lo, p - 2)
                g.tensor_tensor(wl[p % SPLITS][:, :, :], raw_block(p), wh[p % SPLITS][:, :, :], ALU.subtract
                                ).then_inc(w_lo, 1)

            for b in range(4):
                pool.dma_start(dstate[b].rearrange("p (h v) -> p h v", h=H),
                               state_gla[0, b].rearrange("h p v -> p h v")).then_inc(dst_in[b], 16)
            pool.wait_ge(pool_c, 15)
            for p in range(2, NX - NB + 4):
                low_part(p)
                if p == NB:
                    pool.dma_start(rb[:, :], router_b.partition_broadcast(P).rearrange("p a e -> p (a e)")).then_inc(rb_in, 16)
            for b in range(4, DEC):
                i = b % 4
                pool.wait_ge(d_done, b - 3)
                pool.wait_ge(od_full, b - 3)
                pool.dma_start(gla_sample[0, b - 4].rearrange("h p v -> p h v"),
                               dstate[i].rearrange("p (h v) -> p h v", h=H)).then_inc(dst_out[i], 16)
                low_part(NX - NB + b)
                pool.wait_ge(dst_out[i], 16)
                pool.dma_start(dstate[i].rearrange("p (h v) -> p h v", h=H),
                               state_gla[0, b].rearrange("h p v -> p h v")).then_inc(dst_in[i], 16)
            for p in range(NX, NX + 3):
                low_part(p)
            for b in range(4, DEC):
                pool.wait_ge(d_done, b + 1)
                pool.wait_ge(od_full, b + 1)
                pool.dma_start(gla_sample[0, b].rearrange("h p v -> p h v"),
                               dstate[b % 4].rearrange("p (h v) -> p h v", h=H)).then_inc(dst_out[b % 4], 16)
            low_part(NX + 3)
            pool.wait_ge(s_done, NCH * H)
            pool.dma_start(gla_prompt[0, 0].rearrange("h p v -> p h v"), Sg[:, :, :]).then_inc(stored_early, 16)
            pool.wait_ge(small_done, 4)
            pool.dma_start(small, outs[:, :]).then_inc(stored_early, 16)
            for p in range(NX + 4, NX + NB + 3):
                low_part(p)
            wait_filled(pool, "b17")
            wait_filled(pool, "b16")
            pool.dma_start(ln1[:, 0, :], ln1_g.partition_broadcast(P).rearrange("p a e -> p (a e)")).then_inc(ln_in, 16)
            pool.dma_start(ln1[:, 1, :], ln1_b.partition_broadcast(P).rearrange("p a e -> p (a e)")).then_inc(ln_in, 16)
            for p in range(NX + NB + 3, NSPLIT):
                low_part(p)
            wait_drained(pool, "b07")
            pool.dma_start(ln2[:, 0, :], ln2_g.partition_broadcast(P).rearrange("p a e -> p (a e)")).then_inc(ln2_in, 16)
            pool.dma_start(ln2[:, 1, :], ln2_b.partition_broadcast(P).rearrange("p a e -> p (a e)")).then_inc(ln2_in, 16)
            wait_drained(pool, "wo7")
            g.memset(eo, 0.0).then_inc(eo_zero, 1)
            pool.wait_ge(eo_zero, 1)
            pool.dma_start(eo[0:E, :], b_down[0]).then_inc(bdn_in, 16)
            pool.wait_ge(ln_in, 32)
            pool.wait_ge(y_norm, 1)
            y = x1[0:DEC, 2, :]
            g.tensor_tensor(y, ytok[0:DEC, 2, :], ln1[0:DEC, 0, :], ALU.mult).then_inc(x1_small, 1)
            pool.wait_ge(x1_small, 1)
            g.tensor_tensor(y, y, ln1[0:DEC, 1, :], ALU.add).then_inc(x1_small, 1)
            pool.wait_ge(x1_small, 2)
            pool.wait_ge(stored_early, 32)
            for i, t in enumerate((2, 0, 1)):
                rows = TILES[t][1]
                y = rest[t][0:rows, :]
                if t == 2:
                    pool.wait_ge(xp_hi, 2)
                    g.tensor_tensor(y, x1[0:rows, t, :], xparts[t][0][0:rows, :], ALU.subtract).then_inc(xp_r1_small, 1)
                else:
                    pool.wait_ge(xp_r2, i)
                pool.wait_ge(xp_mid, i + 1)
                g.tensor_tensor(y, y, xparts[t][1][0:rows, :], ALU.subtract).then_inc(xp_r2, 1)
            for i in range(4):
                pool.wait_ge(dst_out[i], 32)

        @block.tensor
        def _(pe):
            mm = nc.tensor.matmul

            def project(name, stage=0):
                p = split_of[name]
                pe.wait_ge(w_hi, p + 1)
                pe.wait_ge(*((w_lo_first, p + 1) if p < 2 else (w_lo, p - 1)))
                open_job(pe, name)
                h, l = wh[p % SPLITS], wl[p % SPLITS]
                for k in range(NB):
                    if name in ("xr0", "b10", "b00", "wo0"):
                        pe.wait_ge(x_lo, stage * NB + k + 1)
                    for w, x in ((h, xh[:, k, :]), (h, xl[k]), (l, xh[:, k, :])):
                        last = mm(bank(name)[:, 0:T], w[:, k, :], x, start=(k == 0 and w is h and x is not xl[k]),
                                  stop=(k == NB - 1 and w is l))
                last.then_inc(fl(name), 1)

            def turn(name, pieces):
                open_job(pe, name)
                for out, in_ in pieces:
                    rows = in_.shape[0]
                    last = nc.tensor.transpose(out, in_, ident[0:rows, 0:rows])
                last.then_inc(fl(name), 1)

            for n in range(NB):
                project(f"xr{n}")
            pe.wait_ge(x_landed, 16)
            open_job(pe, "low")
            pe.wait_ge(low_in, 16)
            for k in range(NB):
                last = mm(bank("low")[0:RANK, 0:T], low_w[:, k, :], x_raw[:, k, :], start=(k == 0), stop=(k == NB - 1))
            last.then_inc(fl("low"), 1)
            for n in range(H):
                project(f"k{n}")
            pe.wait_ge(gate_in, 32)
            for n in range(NB):
                pe.wait_ge(conv_done, n + 1)
                for w, name in enumerate((f"r{n}", f"i{n}")):
                    open_job(pe, name)
                    mm(bank(name)[:, 0:T], gate_w[:, w, n, :], xc[:, n, :], start=True, stop=True).then_inc(fl(name), 1)
            for n in range(H):
                project(f"q{n}")
            for n in range(NB):
                project(f"v{n}")
            wait_drained(pe, "low")
            pe.wait_ge(a2_in, 16)
            for h in range(H):
                open_job(pe, f"z{h}")
                mm(bank(f"z{h}")[:, 0:T], a2[:, h * DK:(h + 1) * DK], lowT[:, :], start=True, stop=True
                   ).then_inc(fl(f"z{h}"), 1)
            for n in range(NB):
                project(f"g{n}")
            pe.wait_ge(pool_c, 10)
            for n in range(NB):
                wait_drained(pe, f"v{n}")
            for t, (first, rows) in enumerate(TILES):
                for s in range(2):
                    name = f"vt{t}{s}"
                    turn(name, [(bank(name)[0:rows, c * P:(c + 1) * P], vT[:, 4 * s + c, first:first + rows])
                                for c in range(4)])
            pe.wait_ge(gla_in, 4)
            for t, (first, rows) in enumerate(TILES):
                name = f"kt{t}"
                turn(name, [(bank(name)[0:rows, h * DK:(h + 1) * DK], kd[:, h, first:first + rows]) for h in range(H)])
            open_job(pe, "sc")
            for c in range(NCH):
                p0, cols = (c % 2) * CH, slice(c * CH, (c + 1) * CH)
                for h in range(H):
                    g = 2 * h + c // 2
                    last = mm(bank("sc")[p0:p0 + CH, g * CH:(g + 1) * CH], ke[:, h, cols], qe[:, h, cols],
                              start=True, stop=True)
            last.then_inc(fl("sc"), 1)

            def chunk(c):
                t, p0, cols = c // 2, (c % 2) * CH, slice(c * CH, (c + 1) * CH)
                rows = slice(p0, p0 + CH)
                if c == 2:
                    pe.wait_ge(o_read, 1)
                for h in range(H):
                    out = ob[rows, h // 2, (h % 2) * DV:(h % 2 + 1) * DV]
                    if c:
                        pe.wait_ge(s_done, (c - 1) * H + h + 1)
                    last = mm(out, scs[rows, 2 * h + t, :], vtok[rows, t, h * DV:(h + 1) * DV],
                              start=True, stop=(c == 0))
                    if c:
                        last = mm(out, qe[:, h, cols], Sg[:, h, :], start=False, stop=True)
                last.then_inc(o_full, 1)
                for h in range(H):
                    if c and h % 2 == 0:
                        pe.wait_ge(s_done, (c - 1) * H + h + 2)
                    last = mm(ub[:, h // 2, (h % 2) * DV:(h % 2 + 1) * DV], kdt[rows, t, h * DK:(h + 1) * DK],
                              vtok[rows, t, h * DV:(h + 1) * DV], start=True, stop=True)
                    if h % 2:
                        last.then_inc(u_full, 1)

            for name in [f"vt{t}{s}" for t in range(NT) for s in range(2)] + [f"kt{t}" for t in range(NT)] + ["sc"]:
                wait_drained(pe, name)
            for c in range(NCH):
                chunk(c)
                project(f"m{2 * c}")
                project(f"m{2 * c + 1}")
            pe.wait_ge(o_read, 2)
            for b in range(DEC):
                pe.wait_ge(km_done, b + 1)
                pe.wait_ge(s_done, NCH * H)
                if b:
                    pe.wait_ge(d_done, b)
                for h in range(H):
                    last = mm(ub[:, h // 2, (h % 2) * DV:(h % 2 + 1) * DV], km[:, b % 2, h * DK:(h + 1) * DK],
                              vtok[0:DEC, 2, h * DV:(h + 1) * DV], start=True, stop=True)
                last.then_inc(d_full, 1)
                project(f"m{NB + b}")
                pe.wait_ge(d_done, b + 1)
                for h in range(H):
                    last = mm(ob[0:DEC, h // 2, (h % 2) * DV:(h % 2 + 1) * DV], qd[:, h, b, :],
                              dstate[b % 4][:, h * DV:(h + 1) * DV], start=(b == 0 and h % 2 == 0), stop=True,
                              skip_group_check=True)
                last.then_inc(od_full, 1)
            pe.wait_ge(rg_done, 2)
            for n in range(NB):
                project(f"b1{n}", 1)
            pe.wait_ge(o_norm, NT)
            for n in range(NB):
                name = f"ot{n}"
                turn(name, [(bank(name)[:, first:first + rows], otok[0:rows, t, n * P:(n + 1) * P])
                            for t, (first, rows) in enumerate(TILES)])
            for n in range(NB):
                project(f"b0{n}", 2)
            for s in range(2):
                for n in (range(6), range(6, NB))[s]:
                    project(f"wo{n}", 3)
                if s == 1:
                    wait_filled(pe, "wo7")
                    pe.wait_ge(od_full, DEC)
                    pe.sem_inc(gu_used, NB)
                    pe.sem_inc(dn_used, NB)
                for n in range(4 * s, 4 * s + 4):
                    wait_drained(pe, f"wo{n}")
                for t, (first, rows) in enumerate(TILES):
                    name = f"yt{t}{s}"
                    turn(name, [(bank(name)[0:rows, c * P:(c + 1) * P], yT[:, 4 * s + c, first:first + rows])
                                for c in range(4)])
            pe.wait_ge(y_norm, NT)
            def logits(k):
                wait_drained(pe, f"xt{k}")
                return mm(ob[0:E, 0, 0:T], router_w[:, k, :], x1T[:, k, :], start=(k == 0), stop=(k == NB - 1))

            for n in range(NB):
                name = f"xt{n}"
                turn(name, [(bank(name)[:, first:first + rows], ytok[0:rows, t, n * P:(n + 1) * P])
                            for t, (first, rows) in enumerate(TILES)])
                if n >= 3:
                    logits(n - 3)
            for k in range(NB - 3, NB):
                last = logits(k)
            last.then_inc(lgt_full, 1)
            pe.wait_ge(lgt_read, 1)
            turn("lg", [(bank("lg")[0:rows, t * E:(t + 1) * E], lgT[:, first:first + rows])
                        for t, (first, rows) in enumerate(TILES)])
            pe.wait_ge(sel_done, 2)
            open_job(pe, "rk")
            for t in range(NT):
                for s in range(t + 1):
                    mm(bank("rk")[:, t * E:(t + 1) * E], (before16 if s == t else ones16)[:, :], sel16[:, s, :],
                       start=(s == 0), stop=(s == t))
            for s in range(NT):
                last = mm(bank("rk")[:, NT * E:(NT + 1) * E], ones16[:, :], sel16[:, s, :], start=(s == 0), stop=(s == NT - 1))
            last.then_inc(fl("rk"), 1)

            def gather():
                for n in range(NB):
                    for t in range(NT):
                        for part in range(3):
                            last = mm(GATH[:, n // 4, n % 4 * P:(n % 4 + 1) * P], xparts[t][part][:, n * P:(n + 1) * P],
                                      pick[:, t, :], start=(t == 0 and part == 0), stop=(t == NT - 1 and part == 2))
                last.then_inc(gath_done, 1)

            def turn_weights(done):
                for t, (first, rows) in enumerate(TILES):
                    last = nc.tensor.transpose(SCAT[:, 0, first:first + rows], wpick[0:rows, t, :],
                                               ident[0:rows, 0:rows])
                last.then_inc(done, 1)

            pe.wait_ge(xp_lo, NT)
            pe.wait_ge(picked, 1)
            gather()
            wait_drained(pe, "rk")
            pe.wait_ge(bdn_in, 16)

            def body(it, pair):
                for j in range(2):
                    n = it * 2 + j
                    if j == 0:
                        pe.wait_ge(xg_ready, it + 1)
                    pe.wait_ge(gu_read, n + 1)
                    pe.wait_ge(oh_ready, n + 1)
                    quarters = [((GATE, UP)[f // 2][f % 2 * CAP:(f % 2 + 1) * CAP, :], slice(f * HF, (f + 1) * HF))
                                for f in range(4)]
                    for out, cols in quarters:
                        mm(out, oh[:, :], b3[:, cols], start=True, stop=False)
                    for k in range(NB):
                        pe.wait_ge(gu_in[k], n * 16 + 16)
                        for out, cols in quarters:
                            last = mm(out, xg[:, k, j * CAP:(j + 1) * CAP], gu_w[:, k, cols],
                                      start=False, stop=(k == NB - 1))
                        last.then_inc(gu_used, 1)
                    if j == 0:
                        pe.wait_ge(wpicked, it + 1)
                        pe.wait_ge(scat_read, it * 5 + 1)
                        turn_weights(scat_done)
                        pe.wait_ge(eo_ready, n + 1)
                        for d in range(4):
                            pe.wait_ge(scat_read, it * 5 + 2 + max(d - 1, 0))
                            for x in range(2):
                                last = mm((SCAT, SCAT2)[d % 2][:, x, 0:T], eo[:, (2 * d + x) * P:(2 * d + x + 1) * P],
                                          swT, start=True, stop=True)
                            last.then_inc(scat_done, 1)
                    else:
                        pe.wait_ge(picked, it + 2)
                        pe.wait_ge(scat_read, it * 5 + 6)
                        gather()
                    pe.wait_ge(act_ready, n + 1)
                    for c in range(4):
                        last = nc.tensor.transpose(ACTT[:, c * P:(c + 1) * P], act_s[:, c * P:(c + 1) * P], ident[:, :])
                    last.then_inc(act_tr, 1)
                    pe.wait_ge(actt_ready, n + 1)
                    pe.wait_ge(eo_ready, n + 1)
                    for k in range(NB):
                        pe.wait_ge(dn_in[k], n * 16 + 16)
                        for s in range(2):
                            last = mm(DOWN[s * CAP:(s + 1) * CAP, :], act_t[:, k % 4, k // 4 * CAP:(k // 4 + 1) * CAP],
                                      dn_w[:, k, s * HF:(s + 1) * HF], start=(k == 0), stop=(k == NB - 1))
                        last.then_inc(dn_used, 1)

            moe_loops(pe, body)
            pe.wait_ge(moe_done, 1)
            turn_weights(scat_last)
            u = 0
            for t, (first, rows) in enumerate(TILES):
                for s in range(2):
                    if u >= 2:
                        pe.wait_ge(fin_read, u - 1)
                    for c in range(4):
                        last = nc.tensor.transpose(pool4[0:rows, u % 2, c * P:(c + 1) * P],
                                                   yacc[:, 4 * s + c, first:first + rows], ident[:, :])
                    last.then_inc(fin_full, 1)
                    u += 1
            pe.wait_ge(swt_last, 1)
            pe.wait_ge(eo_last, 1)
            for u in range(2 * NT):
                first, rows = TILES[u // 2]
                mm(last_bank[u][0:rows, :], swT[:, first:first + rows], eo[:, u % 2 * 512:(u % 2 + 1) * 512],
                   start=True, stop=True).then_inc(last_full, 1)

        @block.scalar
        def _(sc):
            me = Steps(sc, act)
            a = nc.scalar.activation
            def high_part(p):
                if p >= NSPLIT:
                    return
                if p >= SPLITS:
                    wait_filled(sc, split_jobs[p - SPLITS])
                wait_raw(sc, p)
                nc.scalar.copy(wh[p % SPLITS][:, :, :], raw_block(p)).then_inc(w_hi, 1)

            def after(name):
                high_part(split_of[name] + SPLITS)

            def high_operand(k, src):
                nc.scalar.copy(xh[:, k, :], src[:, k, :]).then_inc(x_hi, 1)

            sc.wait_ge(x_landed, 16)
            for k in range(NB):
                high_operand(k, x_raw)
            for p in range(SPLITS):
                high_part(p)
            sc.wait_ge(pack_in, 16)
            me.done(a(sp_[:, 0, :], con("lam"), ACT.Abs))
            me.settle()
            me.done(a(sp_[:, 0, :], sp_[:, 0, :], ACT.Exp, scale=-1.0))
            me.settle()
            a(sp_[:, 1, :], sp_[:, 0, :], ACT.Ln, bias=1.0).then_inc(z_ln, 1)
            for n in range(NB):
                wait_filled(sc, f"xr{n}")
                nc.scalar.copy(cin[:, n, CW - 1:CW - 1 + SEQ], bank(f"xr{n}")[:, 0:SEQ])
                nc.scalar.copy(cin[:, n, 2 * (CW - 1) + SEQ:CIN:CW], bank(f"xr{n}")[:, SEQ:T]).then_inc(dr(f"xr{n}"), 1)
                after(f"xr{n}")
            wait_filled(sc, "low")
            nc.scalar.copy(lowT[:, :], bank("low")[0:RANK, 0:T]).then_inc(dr("low"), 1)
            for h in range(H):
                wait_filled(sc, f"k{h}")
                nc.scalar.copy(kT[:, h, :], bank(f"k{h}")[:, 0:T]).then_inc(dr(f"k{h}"), 1)
                after(f"k{h}")
            for n in range(NB):
                for name, dst, bias in ((f"r{n}", rgate, "b_r"), (f"i{n}", igate, "b_i")):
                    wait_filled(sc, name)
                    a(dst[:, n, :], bank(name)[:, 0:T], ACT.Sigmoid, bias=con(bias)[:, n:n + 1]).then_inc(dr(name), 1)
            for h in range(H):
                wait_filled(sc, f"q{h}")
                nc.scalar.mul(qT[:, h, :], bank(f"q{h}")[:, 0:T], DK ** -0.5).then_inc(dr(f"q{h}"), 1)
                after(f"q{h}")
            sc.wait_ge(z_min, 1)
            for n in range(NB):
                wait_drained(sc, f"r{n}")
            for n in range(NB):
                a(decay[:, n, :], rgate[:, n, :], ACT.Exp, scale=sp_[:, 3, n:n + 1]).then_inc(rg_exp, 1)
            after("v0")
            for n in range(NB):
                a(rgate[:, n, :], rgate[:, n, :], ACT.Tanh, scale=sp_[:, 4, n:n + 1]).then_inc(rg_exp, 1)
                if n == 4:
                    after("v1")
            for n in range(4):
                wait_filled(sc, f"v{n}")
                nc.scalar.copy(vT[:, n, :], bank(f"v{n}")[:, 0:T]).then_inc(dr(f"v{n}"), 1)
                if n >= 2:
                    after(f"v{n}")
            sc.wait_ge(rg_root, 1)
            a(root, root, ACT.Sqrt).then_inc(rg_rooted, 1)
            for n in range(4, NB):
                wait_filled(sc, f"v{n}")
                nc.scalar.copy(vT[:, n, :], bank(f"v{n}")[:, 0:T]).then_inc(dr(f"v{n}"), 1)
                after(f"v{n}")
            sc.wait_ge(rg_done, 2)
            for h in range(H):
                wait_filled(sc, f"z{h}")
                a(zb[:, h, :], bank(f"z{h}")[:, 0:T], ACT.Abs, bias=con("b_a")[:, h:h + 1]).then_inc(z_abs, 1)
            sc.wait_ge(z_abs, H)
            me.done(a(zb, zb, ACT.Exp, scale=-1.0))
            me.settle()
            a(zb, zb, ACT.Ln, bias=1.0).then_inc(z_ln, 1)
            after("g0")
            sc.wait_ge(b_done, 1)
            a(eb, bc, ACT.Exp, scale=1.0 / 16).then_inc(b_exp, 1)
            a(enb, bc, ACT.Exp, scale=-1.0 / 16).then_inc(b_exp, 1)
            after("g1")
            sc.wait_ge(b_done, 2)
            a(zb[:, :, 0:SEQ], zb[:, :, 0:SEQ], ACT.Exp, scale=-1.0 / 16).then_inc(b_exp, 1)
            for n in range(NB):
                wait_filled(sc, f"g{n}")
                a(gT[:, n, :], bank(f"g{n}")[:, 0:T], ACT.Sigmoid).then_inc(gsig, 1)
                if n >= 2:
                    after(f"g{n}")
            for t, (first, rows) in enumerate(TILES):
                for s in range(2):
                    name = f"vt{t}{s}"
                    wait_filled(sc, name)
                    nc.scalar.copy(vtok[0:rows, t, s * 512:(s + 1) * 512], bank(name)[0:rows, :]).then_inc(dr(name), 1)

            def merge_gate(n):
                wait_filled(sc, f"m{n}")
                dst = mgla[:, n, :] if n < NB else mrg[:, n - NB, :]
                a(dst, bank(f"m{n}")[:, 0:T], ACT.Sigmoid, bias=con("b_merge")[:, n:n + 1]).then_inc(dr(f"m{n}"), 1)
                after(f"m{n}")

            sc.wait_ge(gla_in, 5)
            for name in ("kt0", "kt1", "kt2"):
                wait_filled(sc, name)
            for c in range(NCH):
                if c % 2 == 1:
                    sc.wait_ge(o_full, c + 1)
                    nc.scalar.copy(otok[:, c // 2, :], ob[:, :, :].rearrange("p a n -> p (a n)")).then_inc(o_read, 1)
                merge_gate(2 * c)
                merge_gate(2 * c + 1)
            sc.wait_ge(braw_in, 48)
            for b in range(DEC):
                merge_gate(NB + b)
                if b < 3:
                    sc.wait_ge(*((pool_c, 15), (b_rest, 1), (b_rest, 2))[b])
                    r = slice(0, (3 - b) * E)
                    nc.scalar.copy(b3[r, :], braw[r, :]).then_inc(b3_step, 1)
            wait_filled(sc, f"m{2 * NB - 1}")
            for k in range(NB):
                high_operand(k, hs)
            sc.wait_ge(od_full, DEC)
            nc.scalar.copy(otok[0:DEC, 2, :], ob[0:DEC, :, :].rearrange("p a n -> p (a n)")).then_inc(od_sb, 1)
            sc.wait_ge(o_var, 1)
            a(rs[:, 0, 0:2 * H], rs[:, 0, 0:2 * H], ACT.Sqrt).then_inc(o_std, 1)
            for n in range(3):
                after(f"b1{n}")
            sc.wait_ge(o_var, 2)
            a(rs[0:DEC, 0, 2 * H:3 * H], rs[0:DEC, 0, 2 * H:3 * H], ACT.Sqrt).then_inc(o_std, 1)
            for n in range(3, NB):
                after(f"b1{n}")
            for n in range(NB):
                wait_drained(sc, f"ot{n}")
                high_operand(n, oT)
            for n in range(NB):
                after(f"b0{n}")
            for n in range(NB):
                wait_drained(sc, f"b0{n}")
                high_operand(n, merged)
            for n in range(NB - 3):
                after(f"wo{n}")
            for s in range(2):
                for t, (first, rows) in enumerate(TILES):
                    name = f"yt{t}{s}"
                    wait_filled(sc, name)
                    nc.scalar.copy(ytok[0:rows, t, s * 512:(s + 1) * 512], bank(name)[0:rows, :]).then_inc(dr(name), 1)
            sc.wait_ge(y_var, 1)
            a(rs1[:, 0, :], rs1[:, 0, :], ACT.Sqrt).then_inc(y_std, 1)

            def x1_hi(t):
                rows = TILES[t][1]
                if t == 2:
                    sc.wait_ge(x1_small, 2)
                    sc.wait_ge(xp_zero, 3)
                else:
                    sc.wait_ge(x1_done, t + 1)
                nc.scalar.copy(xparts[t][0][0:rows, :], x1[0:rows, t, :]).then_inc(xp_hi, 1)

            def x1_mid(t):
                rows = TILES[t][1]
                if t == 2:
                    sc.wait_ge(xp_r1_small, 1)
                else:
                    sc.wait_ge(xp_r1, t + 1)
                nc.scalar.copy(xparts[t][1][0:rows, :], rest[t][0:rows, :]).then_inc(xp_mid, 1)

            for n in range(NB):
                wait_filled(sc, f"xt{n}")
                a(x1T[:, n, :], bank(f"xt{n}")[:, 0:T], ACT.Identity, bias=con("ln1_b")[:, n:n + 1],
                  scale=con("ln1_g")[:, n:n + 1]).then_inc(dr(f"xt{n}"), 1)
                if n in (4, 5, 6):
                    x1_hi({4: 0, 5: 2, 6: 1}[n])
            x1_mid(2)
            x1_mid(0)
            sc.wait_ge(lgt_full, 1)
            nc.scalar.copy(lgT, ob[0:E, 0, 0:T]).then_inc(lgt_read, 1)
            x1_mid(1)
            for i, t in enumerate((2, 0, 1)):
                rows = TILES[t][1]
                sc.wait_ge(xp_r2, i + 1)
                nc.scalar.copy(xparts[t][2][0:rows, :], rest[t][0:rows, :]).then_inc(xp_lo, 1)
            sc.wait_ge(lg_done, 1)
            a(ex[:, :, :], ex[:, :, :], ACT.Exp).then_inc(ex_done, 1)
            sc.wait_ge(gath_done, 1)
            nc.scalar.copy(xg, GATH[:, :, :].rearrange("p a n -> p (a n)").rearrange("p (n c) -> p n c", n=NB)
                           ).then_inc(xg_ready, 1)
            nc.scalar.copy(rs[0:1, 0, 0:1], ident[0:1, 0:1]).then_inc(eo_ready, 1)

            def body(it, pair):
                for j in range(2):
                    n = it * 2 + j
                    sc.wait_ge(gclip, n + 1)
                    a(sbuf_, gbuf, ACT.Sigmoid, scale=SWISH).then_inc(sig_done, 1)
                    sc.wait_ge(act_tr, n + 1)
                    nc.scalar.copy(act_t, ACTT.rearrange("p (c s) -> p c s", c=4)).then_inc(actt_ready, 1)
                    if j == 1:
                        sc.wait_ge(gath_done, it + 2)
                        nc.scalar.copy(xg, GATH[:, :, :].rearrange("p a n -> p (a n)").rearrange("p (n c) -> p n c", n=NB)
                                       ).then_inc(xg_ready, 1)
                    sc.wait_ge(dn_used, n * NB + 2 * NB)
                    sc.wait_ge(scat_done, it * 5 + 5)
                    for s in range(2):
                        last = nc.scalar.copy(eo[j * CAP:(j + 1) * CAP, s * HF:(s + 1) * HF],
                                              DOWN[s * CAP:(s + 1) * CAP, :])
                    last.then_inc(eo_ready, 1)

            moe_loops(sc, body)
            nc.scalar.copy(rs[0:1, 0, 1:2], ident[0:1, 0:1]).then_inc(eo_last, 1)
            for t, (first, rows) in enumerate(TILES):
                sc.wait_ge(y2_var, t + 1)
                a(rs1[0:rows, 0, t:t + 1], rs1[0:rows, 0, t:t + 1], ACT.Sqrt).then_inc(y2_std, 1)

        @block.vector
        def _(v):
            me = Steps(v, dve)
            V = nc.vector
            stt, tt, ts = V.scalar_tensor_tensor, V.tensor_tensor, V.tensor_scalar
            def low_operand(k, src, stage):
                v.wait_ge(x_hi, stage * NB + k + 1)
                tt(xl[k], src[:, k, :], xh[:, k, :], ALU.subtract).then_inc(x_lo, 1)

            for k in range(NB):
                low_operand(k, x_raw, 0)
            for p in range(2):
                v.wait_ge(w_hi, p + 1)
                tt(wl[p][:, :, :], raw_block(p), wh[p][:, :, :], ALU.subtract).then_inc(w_lo_first, 1)
            me.done(V.memset(cin[:, :, 0:CW - 1], 0.0))
            v.wait_ge(pack_in, 16)
            me.done(V.tensor_copy(cin[:, :, CW - 1 + SEQ:CIN].rearrange("p n (b f) -> p n b f", f=CW)[:, :, :, 0:CW - 1],
                                  con("conv0").rearrange("p (n b f) -> p n b f", n=NB, b=DEC)))
            me.settle()
            me.done(ts(sp_[:, 2, :], con("lam"), -1.0, 0.0, ALU.mult, ALU.max))
            me.settle()
            v.wait_ge(z_ln, 1)
            me.done(tt(sp_[:, 2, :], sp_[:, 2, :], sp_[:, 1, :], ALU.add))
            me.settle()
            me.done(ts(sp_[:, 3, :], sp_[:, 2, :], -8.0, None, ALU.mult))
            ts(sp_[:, 4, :], sp_[:, 2, :], 8.0, None, ALU.mult).then_inc(z_min, 1)
            for n in range(NB):
                wait_drained(v, f"xr{n}")
                w = lambda j: conv_w[:, n, j:j + 1]
                tmp = ctmp[:, 0, :]
                me.settle()
                if n:
                    v.wait_ge(conv_done, n)
                me.done(ts(tmp, cin[:, n, 0:COUT], w(0), conv_b[:, n:n + 1], ALU.mult, ALU.add))
                me.settle()
                for j in range(1, CW - 1):
                    nxt = ctmp[:, j % 2, :]
                    me.done(stt(nxt, cin[:, n, j:j + COUT], w(j), tmp, ALU.mult, ALU.add))
                    me.settle()
                    tmp = nxt
                me.done(stt(xc[:, n, SEQ:T], cin[:, n, SEQ + 2 * (CW - 1):CIN:CW], w(CW - 1),
                            tmp[:, SEQ + CW - 1:COUT:CW], ALU.mult, ALU.add))
                stt(xc[:, n, 0:SEQ], cin[:, n, CW - 1:CW - 1 + SEQ], w(CW - 1), tmp[:, 0:SEQ], ALU.mult, ALU.add
                    ).then_inc(conv_done, 1)
            v.wait_ge(conv_done, NB)
            V.tensor_copy(outs[:, OUT_CONVP:OUT_CONVS].rearrange("p (n f) -> p n f", n=NB),
                          cin[:, :, SEQ:SEQ + CW - 1]).then_inc(small_done, 1)
            V.tensor_copy(outs[:, OUT_CONVS:OUT_HP].rearrange("p (n b f) -> p n b f", n=NB, b=DEC),
                          cin[:, :, CW - 1 + SEQ:CIN].rearrange("p n (b f) -> p n b f", f=CW)[:, :, :, 1:CW]
                          ).then_inc(small_done, 1)
            v.wait_ge(rg_exp, NB)
            me.done(tt(root, decay, decay, ALU.mult))
            me.settle()
            v.wait_ge(rg_exp, 2 * NB)
            stt(root, root, 1.0, rgate, ALU.add, ALU.mult).then_inc(rg_root, 1)
            for n in range(NB):
                wait_drained(v, f"i{n}")
            me.done(tt(igate, igate, xc, ALU.mult))
            me.settle()
            v.wait_ge(rg_rooted, 1)
            me.done(tt(igate, igate, root, ALU.mult))
            me.settle()
            h0 = blocks(con("h0"), NB)
            me.done(tt(hs[:, :, SEQ:T], decay[:, :, SEQ:T], h0, ALU.mult))
            me.settle()
            me.done(tt(hs[:, :, SEQ:T], hs[:, :, SEQ:T], igate[:, :, SEQ:T], ALU.add))
            for n in range(NB):
                me.done(V.tensor_tensor_scan(hs[:, n, 0:SEQ], decay[:, n, 0:SEQ], igate[:, n, 0:SEQ], 0.0,
                                             ALU.mult, ALU.add))
            me.settle()
            V.tensor_copy(outs[:, OUT_HP:OUT_HS].rearrange("p (n f) -> p n f", f=1), hs[:, :, SEQ - 1:SEQ]
                          ).then_inc(small_done, 1)
            V.tensor_copy(blocks(outs[:, OUT_HS:NOUT], NB), hs[:, :, SEQ:T]).then_inc(small_done, 1)
            v.wait_ge(small_done, 4)
            V.memset(mx[:, :, :], 0.0).then_inc(rg_done, 1)
            V.memset(lg[:, :, :], 0.0).then_inc(rg_done, 1)
            for h in range(H):
                v.wait_ge(z_abs, h + 1)
                ts(za[:, h, :], bank(f"z{h}")[:, 0:T], con("b_a")[:, h:h + 1], 0.0, ALU.add, ALU.min
                   ).then_inc(dr(f"z{h}"), 1)
            for h in range(H):
                wait_drained(v, f"z{h}")
            v.wait_ge(z_ln, 2)
            me.done(tt(za, za, zb, ALU.subtract))
            me.settle()
            v.wait_ge(pool_c, 10)
            for h in range(H):
                me.done(V.tensor_tensor_scan(bc[:, h, :], keep[:, :], za[:, h, :], 0.0, ALU.mult, ALU.add))
            me.settle()
            bcc = bc[:, :, 0:SEQ].rearrange("p h (c t) -> p h c t", c=NCH)
            V.tensor_copy(ebl[:, :, :], bcc[:, :, :, CH - 1]).then_inc(b_done, 1)
            v.wait_ge(b_done, 1)
            tt(zb[:, :, 0:SEQ].rearrange("p h (c t) -> p h c t", c=NCH), bcc,
               ebl[:, :, :].unsqueeze(3).to_broadcast([P, H, NCH, CH]), ALU.subtract).then_inc(b_done, 1)
            v.wait_ge(b_exp, 2)
            tt(qe, qT, eb, ALU.mult).then_inc(gla_in, 1)
            tt(ke, kT, enb, ALU.mult).then_inc(gla_in, 1)
            v.wait_ge(b_exp, 3)
            tt(kd[:, :, 0:SEQ], kT[:, :, 0:SEQ], zb[:, :, 0:SEQ], ALU.mult).then_inc(gla_in, 1)
            V.tensor_copy(kd[:, :, SEQ:T], kT[:, :, SEQ:T]).then_inc(gla_in, 1)
            v.wait_ge(b_done, 2)
            me.done(V.tensor_copy(ebl[:, :, :], eb[:, :, CH - 1:SEQ:CH]))
            me.done(V.memset(qd, 0.0))
            me.settle()
            me.done(V.tensor_copy(keep[:, 0:H * DEC * DEC].rearrange("p (h c) -> p h c", h=H)[:, :, 0:DEC * DEC:DEC + 1],
                                  qT[:, :, SEQ:T]))
            V.tensor_copy(ebd[:, :, :], eb[:, :, SEQ:T]).then_inc(gla_in, 1)
            for n in range(NB):
                v.wait_ge(gsig, n + 1)
                stt(gT[:, n, :], bank(f"g{n}")[:, 0:T], con("norm_g")[:, n:n + 1], gT[:, n, :], ALU.mult, ALU.mult
                    ).then_inc(dr(f"g{n}"), 1)
            for t, (first, rows) in enumerate(TILES):
                name = f"kt{t}"
                wait_filled(v, name)
                V.tensor_copy(kdt[0:rows, t, :], bank(name)[0:rows, :]).then_inc(dr(name), 1)
            wait_filled(v, "sc")
            tt(scs, bank("sc").rearrange("p (g t) -> p g t", t=CH),
               causal[:, :].unsqueeze(1).to_broadcast([P, 8, CH]), ALU.mult).then_inc(dr("sc"), 1)
            wait_drained(v, "kt2")

            def k_row(b):
                ts(km[:, b % 2, :], kdt[0:DEC, 2, :], ident[0:DEC, b:b + 1], None, ALU.mult).then_inc(km_done, 1)

            k_row(0)
            k_row(1)
            me.settle()
            v.wait_ge(gla_in, 5)
            for c in range(NCH):
                for h in range(H):
                    if h % 2 == 0:
                        v.wait_ge(u_full, c * 2 + h // 2 + 1)
                    if h == 0:
                        v.wait_ge(o_full, c + 1)
                        if c:
                            v.wait_ge(s_done, c * H)
                    u = ub[:, h // 2, (h % 2) * DV:(h % 2 + 1) * DV]
                    if c:
                        stt(Sg[:, h, :], Sg[:, h, :], ebl[:, h, c:c + 1], u, ALU.mult, ALU.add).then_inc(s_done, 1)
                    else:
                        V.tensor_copy(Sg[:, h, :], u).then_inc(s_done, 1)

            def norm_stats(tiles_):
                for t in tiles_:
                    rows = TILES[t][1]
                    for h in range(H):
                        me.done(V.bn_stats(st[0:rows, t, h, :], otok[0:rows, t, h * DV:(h + 1) * DV]))
                me.settle()
                for t in tiles_:
                    rows = TILES[t][1]
                    for h in range(H):
                        me.done(V.bn_aggr(mv[0:rows, t, h, :], st[0:rows, t, h, :]))
                me.settle()
                a, b, rows = tiles_[0], tiles_[-1] + 1, TILES[tiles_[0]][1]
                ts(rs[0:rows, 0, a * H:b * H].rearrange("p (t h) -> p t h", h=H), mv[0:rows, a:b, :, 1], EPS, None, ALU.add
                   ).then_inc(o_var, 1)

            for b in range(DEC):
                v.wait_ge(dst_in[b % 4], 16 * (b // 4 + 1))
                v.wait_ge(d_full, b + 1)
                for h in range(H):
                    sl = dstate[b % 4][:, h * DV:(h + 1) * DV]
                    last = stt(sl, sl, ebd[:, h, b:b + 1], ub[:, h // 2, (h % 2) * DV:(h % 2 + 1) * DV], ALU.mult, ALU.add)
                last.then_inc(d_done, 1)
                if b in (1, 2):
                    v.wait_ge(b3_step, b)
                    r = slice(0, (3 - b) * E)
                    tt(braw[r, :], braw[r, :], b3[r, :], ALU.subtract).then_inc(b_rest, 1)
                if b + 2 < DEC:
                    k_row(b + 2)
            for k in range(NB):
                low_operand(k, hs, 1)
            v.wait_ge(o_read, 2)
            norm_stats([0, 1])

            def normalise(t):
                rows = TILES[t][1]
                for h in range(H):
                    o = otok[0:rows, t, h * DV:(h + 1) * DV]
                    last = ts(o, o, mv[0:rows, t, h, 0:1], rs[0:rows, 1, t * H + h:t * H + h + 1], ALU.subtract, ALU.mult)
                last.then_inc(o_norm, 1)

            v.wait_ge(o_std, 1)
            me.done(V.reciprocal(rs[:, 1, 0:2 * H], rs[:, 0, 0:2 * H]))
            me.settle()
            normalise(0)
            normalise(1)
            for n in range(NB):
                if n == 3:
                    v.wait_ge(od_sb, 1)
                    norm_stats([2])
                if n == 5:
                    v.wait_ge(o_std, 2)
                    me.done(V.reciprocal(rs[0:DEC, 1, 2 * H:3 * H], rs[0:DEC, 0, 2 * H:3 * H]))
                    me.settle()
                    normalise(2)
                wait_filled(v, f"b1{n}")
                wait_drained(v, f"m{NB + n}")
                tt(merged[:, n, :], bank(f"b1{n}")[:, 0:T], mrg[:, n, :], ALU.mult).then_inc(dr(f"b1{n}"), 1)
            for n in range(NB):
                wait_drained(v, f"g{n}")
            for n in range(NB):
                wait_filled(v, f"ot{n}")
                tt(oT[:, n, :], bank(f"ot{n}")[:, 0:T], gT[:, n, :], ALU.mult).then_inc(dr(f"ot{n}"), 1)
                if n >= 2:
                    low_operand(n - 2, oT, 2)
            for k in range(NB - 2, NB):
                low_operand(k, oT, 2)
            for n in range(NB):
                wait_drained(v, f"m{n}")
                wait_drained(v, f"b1{n}")
            for n in range(NB):
                wait_filled(v, f"b0{n}")
                me.done(tt(mgla[:, n, :], bank(f"b0{n}")[:, 0:T], mgla[:, n, :], ALU.mult))
                me.settle()
                tt(merged[:, n, :], merged[:, n, :], mgla[:, n, :], ALU.add).then_inc(dr(f"b0{n}"), 1)
            for k in range(NB):
                low_operand(k, merged, 3)
            v.wait_ge(x_again, 16)
            for n in range(NB):
                wait_filled(v, f"wo{n}")
                stt(yT[:, n, :], x_res[:, n, :], ALPHA, bank(f"wo{n}")[:, 0:T], ALU.mult, ALU.add).then_inc(dr(f"wo{n}"), 1)
                if n in (1, 3):
                    V.memset(xparts[2][n // 2], 0.0).then_inc(xp_zero, 1)

            me.done(V.memset(mv1[:, :, :], 1.0))
            me.done(V.tensor_copy(before16[:, :], before[:, :]))
            me.done(V.tensor_copy(ones16[:, :], ones[:, :]))
            for t in (sel, sel16, ex):
                me.done(V.memset(t[:, :, :], 0.0))
            me.done(V.memset(keep3[:, :], 1.0))
            me.settle()
            me.done(V.memset(keep3[:, 0:NT * E:E], 0.0))
            for s in range(2):
                for t, (first, rows) in enumerate(TILES):
                    wait_drained(v, f"yt{t}{s}")
                    me.done(V.bn_stats(st1[0:rows, t, s, :], ytok[0:rows, t, s * 512:(s + 1) * 512]))
            me.settle()
            for t, (first, rows) in enumerate(TILES):
                me.done(V.bn_aggr(mv1[0:rows, t, :], st1[0:rows, t, :, :].rearrange("p a b -> p (a b)")))
            me.settle()
            ts(rs1[:, 0, :], mv1[:, :, 1], EPS, None, ALU.add).then_inc(y_var, 1)
            v.wait_ge(y_std, 1)
            me.done(V.reciprocal(rs1[:, 1, :], rs1[:, 0, :]))
            me.settle()
            for t in (2, 0, 1):
                rows = TILES[t][1]
                ts(ytok[0:rows, t, :], ytok[0:rows, t, :], mv1[0:rows, t, 0:1], rs1[0:rows, 1, t:t + 1],
                   ALU.subtract, ALU.mult).then_inc(y_norm, 1)
            v.wait_ge(ln_in, 32)
            v.wait_ge(y_norm, NT)
            for t in range(2):
                me.done(tt(x1[:, t, :], ytok[:, t, :], ln1[:, 0, :], ALU.mult))
            me.settle()
            for t in range(2):
                tt(x1[:, t, :], x1[:, t, :], ln1[:, 1, :], ALU.add).then_inc(x1_done, 1)
            V.memset(xparts[2][2], 0.0).then_inc(xp_zero, 1)
            for n in range(NB):
                wait_filled(v, f"xt{n}")
            for t, (first, rows) in enumerate(TILES[:2]):
                v.wait_ge(xp_hi, 2 * t + 1)
                tt(ytok[0:rows, t, :], x1[0:rows, t, :], xparts[t][0][0:rows, :], ALU.subtract).then_inc(xp_r1, 1)
            v.wait_ge(rb_in, 16)
            wait_filled(v, "lg")
            me.done(tt(lg[:, 0:2, :], bank("lg")[:, 0:2 * E].rearrange("p (t e) -> p t e", e=E),
                       rb[:, :].unsqueeze(1).to_broadcast([P, 2, E]), ALU.add))
            tt(lg[0:DEC, 2, :], bank("lg")[0:DEC, 2 * E:3 * E], rb[0:DEC, :], ALU.add).then_inc(dr("lg"), 1)
            wait_drained(v, "lg")
            me.settle()
            for t in range(NT):
                me.done(V.max(mx[:, t, :], lg[:, t, :]))
            me.settle()
            fourth = mx[:, :, 3:4].to_broadcast([P, NT, E])
            flat = lambda ap: ap[:, :, :].rearrange("p t e -> p (t e)")
            me.done(tt(eq[:, :, :], lg[:, :, :], fourth, ALU.is_equal))
            me.done(tt(cum2[:, :, :], lg[:, :, :], fourth, ALU.is_gt))
            me.settle()
            me.done(V.tensor_tensor_scan(flat(cum), keep3[:, :], flat(eq), 0.0, ALU.mult, ALU.add))
            me.done(V.reduce_sum(red[:, 1, :], cum2[:, :, :], AX_X))
            me.settle()
            me.done(tt(cum[:, :, :], cum[:, :, :], red[:, 1, :].unsqueeze(2).to_broadcast([P, NT, E]), ALU.add))
            me.settle()
            me.done(stt(flat(eq), flat(cum), 4.0, flat(eq), ALU.is_le, ALU.mult))
            me.settle()
            for s in (sel16, sel):
                tt(s[:, 0:2, :], cum2[:, 0:2, :], eq[:, 0:2, :], ALU.add).then_inc(sel_done, 1)
                tt(s[0:DEC, 2, :], cum2[0:DEC, 2, :], eq[0:DEC, 2, :], ALU.add).then_inc(sel_done, 1)
            v.wait_ge(sel_done, 4)
            tt(ex[:, :, :], lg[:, :, :], mx[:, :, 0:1].to_broadcast([P, NT, E]), ALU.subtract).then_inc(lg_done, 1)
            me.done(ts(eq[:, :, :], sel[:, :, :], -FAR, FAR, ALU.mult, ALU.add))
            me.settle()
            wait_filled(v, "rk")
            me.done(tt(rankx[:, :, 0:E], eq[:, :, :], bank("rk")[:, 0:NT * E].rearrange("p (t e) -> p t e", e=E), ALU.add))
            V.reduce_max(red[:, 0, 0:1], bank("rk")[:, NT * E:(NT + 1) * E], AX_X).then_inc(dr("rk"), 1)
            me.settle()
            iota4 = iota[:, :].unsqueeze(1).unsqueeze(1).to_broadcast([P, NT, 2, CAP])

            def choose(first):
                tt(pick.rearrange("p t (j c) -> p t j c", j=2), iota4,
                   rankx[:, :, first].unsqueeze(3).to_broadcast([P, NT, 2, CAP]), ALU.is_equal).then_inc(picked, 1)

            wait_drained(v, "rk")
            choose(slice(0, 2))
            V.memset(rs[0:1, 1, 0:1], 0.0).then_inc(gu_read, 1)
            V.memset(rs[0:1, 1, 1:2], 0.0).then_inc(scat_read, 1)
            v.wait_ge(pool_c, 15)

            def one_hot(first):
                ts(oh[:, :], which[:, :], eid[:, first], None, ALU.is_equal).then_inc(oh_ready, 1)

            v.wait_ge(b3_step, 3)
            one_hot(slice(0, 1))
            v.wait_ge(ex_done, 1)
            me.done(tt(ex[:, :, :], ex[:, :, :], sel[:, :, :], ALU.mult))
            me.settle()
            me.done(V.reduce_sum(red[:, 1, :], ex[:, :, :], AX_X))
            me.done(V.memset(wpick[:, :, :], 0.0))
            me.done(V.memset(yacc, 0.0))
            me.settle()
            me.done(ts(red[:, 1, :], red[:, 1, :], 1e-30, None, ALU.max))
            me.settle()
            me.done(V.reciprocal(red[:, 3, :], red[:, 1, :]))
            me.settle()
            me.done(tt(wtx[:, :, 0:E], ex[:, :, :], red[:, 3, :].unsqueeze(2).to_broadcast([P, NT, E]), ALU.mult))
            me.settle()
            V.tensor_copy(wpick[:, :, 0:E], wtx[:, :, 0:E]).then_inc(wpicked, 1)
            for p in range(1, PASSES + 1):
                me.done(ts(rankx[:, :, p * E:(p + 1) * E], rankx[:, :, 0:E], -float(CAP * p), None, ALU.add))
            me.settle()
            ts(flag[:, :], red[:, 0, 0:1], float(CAP), None, ALU.is_gt).then_inc(flag_done, 1)
            def body(it, pair):
                me.n, me.base = 0, it * STEP + base
                for j in range(2):
                    n = it * 2 + j
                    e = pair * 2 + j
                    v.wait_ge(gu_used, n * NB + 2 * NB)
                    ts(gbuf, GATE, LIMIT, None, ALU.min).then_inc(gclip, 1)
                    ts(ubuf, UP, LIMIT, -LIMIT, ALU.min, ALU.max).then_inc(gu_read, 1)
                    one_hot(bass.ds(e + 1, 1))
                    if j == 0:
                        v.wait_ge(scat_done, it * 5 + 1)
                        V.tensor_copy(swT, SCAT[:, 0, 0:T]).then_inc(scat_read, 1)
                    v.wait_ge(gclip, n + 1)
                    v.wait_ge(gu_read, n + 2)
                    me.done(stt(tbuf, ubuf, 1.0, gbuf, ALU.add, ALU.mult))
                    me.settle()
                    v.wait_ge(sig_done, n + 1)
                    tt(act_s, tbuf, sbuf_, ALU.mult).then_inc(act_ready, 1)
                    if j == 0:
                        v.wait_ge(scat_read, it * 5 + 2)
                        for d in range(4):
                            v.wait_ge(scat_done, it * 5 + 2 + d)
                            y = yacc[:, 2 * d:2 * d + 2, :]
                            tt(y, y, (SCAT, SCAT2)[d % 2][:, :, 0:T], ALU.add).then_inc(scat_read, 1)
                        tt(wpick.rearrange("p t (j c) -> p t j c", j=2), pick.rearrange("p t (j c) -> p t j c", j=2),
                           wtx[:, :, bass.ds(pair * 2, 2)].unsqueeze(3).to_broadcast([P, NT, 2, CAP]), ALU.mult
                           ).then_inc(wpicked, 1)
                        v.wait_ge(wpicked, it + 2)
                        v.wait_ge(gath_done, it + 1)
                        choose(bass.ds(it * 2 + 2, 2))
                assert me.n == STEP, me.n

            STEP = 2
            base = me.n
            with v.Fori(0, PAIRS) as pair:
                body(pair, pair)
            v.wait_ge(flag_done, 1)
            over = v.value_load(flag[0:1, 0:1], min_val=0, max_val=1)
            with v.If(over == 1):
                with v.Fori(1, PASSES) as turn_:
                    with v.Fori(0, PAIRS) as pair:
                        body(turn_ * PAIRS + pair, pair)
            V.memset(mx[0:1, 0, 0:1], 0.0).then_inc(moe_done, 1)
            me.s, me.n, me.base = tail, 0, 0
            v.wait_ge(ln2_in, 32)
            me.done(V.memset(mv1[:, :, :], 1.0))
            v.wait_ge(scat_last, 1)
            V.tensor_copy(swT, SCAT[:, 0, 0:T]).then_inc(swt_last, 1)
            for u in range(2 * NT):
                t, cols, rows = u // 2, slice(u % 2 * 512, (u % 2 + 1) * 512), TILES[u // 2][1]
                v.wait_ge(fin_full, u + 1)
                stt(y2[0:rows, t, cols], x1[0:rows, t, cols], ALPHA, pool4[0:rows, u % 2, :], ALU.mult, ALU.add
                    ).then_inc(fin_read, 1)

            def finish(t):
                rows = TILES[t][1]
                y = y2[0:rows, t, :]
                me.done(stt(y, y, mv1[0:rows, t, 0:1], ln2[0:rows, 0, :], ALU.subtract, ALU.mult))
                v.wait_ge(y2_std, t + 1)
                me.done(V.reciprocal(rs1[0:rows, 1, t:t + 1], rs1[0:rows, 0, t:t + 1]))
                me.settle()
                stt(y, y, rs1[0:rows, 1, t:t + 1], ln2[0:rows, 1, :], ALU.mult, ALU.add).then_inc(y2_done, 1)

            v.wait_ge(fin_read, 2 * NT)
            for t, (first, rows) in enumerate(TILES):
                for s in range(2):
                    u, y = 2 * t + s, y2[0:rows, t, s * 512:(s + 1) * 512]
                    v.wait_ge(last_full, u + 1)
                    me.done(tt(y, y, last_bank[u][0:rows, :], ALU.add))
                    me.settle()
                    me.done(V.bn_stats(st1[0:rows, t, s, :], y))
                me.settle()
                me.done(V.bn_aggr(mv1[0:rows, t, :], st1[0:rows, t, :, :].rearrange("p a b -> p (a b)")))
                me.settle()
                ts(rs1[0:rows, 0, t:t + 1], mv1[0:rows, t, 1:2], EPS, None, ALU.add).then_inc(y2_var, 1)
                if t:
                    finish(t - 1)
            finish(NT - 1)


_NAMES = ("xT", "w_in", "w_branch", "w_o", "gla_w_a2", "rg_w_a", "rg_w_x", "state_gla", "pack", "moe_b_gu", "ln1_g", "ln1_b",
          "ln2_g", "ln2_b", "router_b", "moe_w_gu", "moe_w_down", "moe_b_down")
_OUTS = (("y_prompt", (1, SEQ, D)), ("y_sample", (DEC, 1, D)), ("gla_prompt", (1, 1, H, DK, DV)),
         ("gla_sample", (1, DEC, H, DK, DV)), ("small", (P, NOUT)))


def kernel(**inputs):
    import numpy as np
    import concourse.bacc as bacc
    from concourse.bass_utils import run_bass_kernel_spmd as run

    x = {k: np.asarray(v) for k, v in inputs.items()}

    def channels(a):
        a = np.moveaxis(a, -1, 0)
        a = a.reshape((-1, P) + a.shape[1:])
        return np.moveaxis(a, 1, 0)

    tokens = np.concatenate([x["x_prompt"][0], x["x_sample"][:, 0]], axis=0)
    parts = {
        "conv_w": channels(x["rg_conv_w"][0]), "conv_b": channels(x["rg_conv_b"][0]),
        "b_r": channels(x["rg_b_a"][0]), "b_i": channels(x["rg_b_x"][0]), "lam": channels(x["rg_lambda"][0]),
        "b_a": channels(x["gla_b_a"][0]), "norm_g": channels(x["gla_norm_g"][0]),
        "b_merge": channels(x["b_merge"][0]), "h0": channels(x["state_rglru"][0]),
        "conv0": channels(x["state_conv"][0]),
        "router_w": channels(np.swapaxes(x["router_w"][0], 0, 1)),
        "ln1_g": channels(x["ln1_g"][0]), "ln1_b": channels(x["ln1_b"][0]),
    }
    x["pack"] = np.concatenate([parts[n].reshape(P, -1) for n in PACK], axis=1)
    x["xT"] = channels(tokens)

    nc = bacc.Bacc("TRN2", target_bir_lowering=False, num_devices=1)
    arrays, args = {}, []
    for name in _NAMES:
        a = np.ascontiguousarray(x[name])
        arrays[f"in_{name}"] = a
        args.append(nc.dram_tensor(f"in_{name}", a.shape, mybir.dt.from_np(a.dtype), kind="ExternalInput").ap())
    for name, shape in _OUTS:
        args.append(nc.dram_tensor(f"out_{name}", shape, F32, kind="ExternalOutput").ap())
    build(nc, *args)
    got = run(nc, [arrays], core_ids=[0]).results[0]
    small = got["out_small"]

    def rows(a, inner):
        a = a.reshape((P, NB) + inner)
        return np.moveaxis(a, (1, 0), (-2, -1)).reshape(inner + (D,))

    conv_p = rows(small[:, OUT_CONVP:OUT_CONVS], (CW - 1,))[None, None]
    conv_s = rows(small[:, OUT_CONVS:OUT_HP], (DEC, CW - 1))[None]
    h_p = rows(small[:, OUT_HP:OUT_HS], (1,))[None]
    h_s = rows(small[:, OUT_HS:NOUT], (DEC,))[None]
    return (got["out_y_prompt"], got["out_y_sample"], got["out_gla_prompt"], h_p, conv_p, got["out_gla_sample"],
            h_s, conv_s)
```
